# Optimizing a Trainium2 kernel written in Bass

```python
import math
import functools
import jax
import jax.numpy as jnp
from jax import lax
import numpy as np

D_MODEL = 1024
BATCH = 1
SEQ = 1024
DEPTH = 2
DEC_BATCH = 8
DEC_SEQ = 8
PAST_LEN = 8192
PAGE_SIZE = 128

HEAD_DIM = 64
A_WIDTH = D_MODEL // 4
B_WIDTH = D_MODEL // 2
C_WIDTH = D_MODEL - A_WIDTH - B_WIDTH
A_HEADS = A_WIDTH // HEAD_DIM
B_HEADS = B_WIDTH // HEAD_DIM
B_KV_HEADS = B_HEADS // 2
C_HEADS = C_WIDTH // HEAD_DIM
MIX_WIDTH = A_WIDTH + B_WIDTH + C_WIDTH
IDX_HEADS = 8
IDX_DIM = 64
TOPK_MAX = 256
Q_BLOCK = 128
ROT_DIM = HEAD_DIM // 4
ROPE_THETA = 500000.0
MLSTM_CHUNK = 64
DECAY_LORA = 64
AAA_LORA = 64
GATE_LORA = 128
RWKV_LN_EPS = 64e-5
NORM_EPS = 1e-6
D_FF = ((8 * D_MODEL + 767) // 768) * 256
A_SPLITS = (A_WIDTH, A_WIDTH, A_WIDTH, A_WIDTH, 2 * A_HEADS)
B_SPLITS = (B_WIDTH, B_KV_HEADS * HEAD_DIM, B_KV_HEADS * HEAD_DIM,
            IDX_HEADS * IDX_DIM, IDX_DIM, IDX_HEADS)
C_SPLITS = (C_WIDTH, C_WIDTH, C_WIDTH, DECAY_LORA, AAA_LORA, GATE_LORA)
A_PROJ = sum(A_SPLITS)
B_PROJ = sum(B_SPLITS)
C_PROJ = sum(C_SPLITS)
P_IN = A_PROJ + B_PROJ + C_PROJ

kernel_name = 'hybrid_mlstm_dsa_rwkv7_decode_step'

def split_cols(a, sizes):
    cuts = [sum(sizes[:i + 1]) for i in range(len(sizes) - 1)]
    return jnp.split(a, cuts, axis=-1)

def rmsnorm(x, g):
    xf = x.astype(jnp.float32)
    y = xf * lax.rsqrt(jnp.mean(xf * xf, axis=-1, keepdims=True) + NORM_EPS)
    return (y * g.astype(jnp.float32)).astype(x.dtype)

def rotary(x, pos):
    half = ROT_DIM // 2
    inv = ROPE_THETA ** (-jnp.arange(half, dtype=jnp.float32) / half)
    ang = pos.astype(jnp.float32)[:, None] * inv[None, :]
    cos = jnp.cos(ang)[None, :, None, :]
    sin = jnp.sin(ang)[None, :, None, :]
    xr = x[..., :ROT_DIM].astype(jnp.float32)
    x1, x2 = xr[..., :half], xr[..., half:]
    rot = jnp.concatenate([x1 * cos - x2 * sin, x2 * cos + x1 * sin], axis=-1).astype(x.dtype)
    return jnp.concatenate([rot, x[..., ROT_DIM:]], axis=-1)

def mlstm_chunkwise(q, k, v, log_i, log_f, C0, n0, m0):
    Bsz, L, H, d = q.shape
    Lc = math.gcd(L, MLSTM_CHUNK)
    nc = L // Lc

    def chunks(a):
        a = a.reshape(Bsz, nc, Lc, H, *a.shape[3:])
        return jnp.moveaxis(jnp.moveaxis(a, 1, 0), 3, 2)

    causal = jnp.tril(jnp.ones((Lc, Lc), dtype=bool))

    def step(carry, inp):
        C, n, m = carry
        qc, kc, vc, ic, fc = inp
        b = jnp.cumsum(fc, axis=-1)
        D = jnp.where(causal, b[..., :, None] - b[..., None, :] + ic[..., None, :], -jnp.inf)
        inter = b + m[..., None]
        m_t = jnp.maximum(inter, jnp.max(D, axis=-1))
        s = jnp.einsum('bhtd,bhsd->bhts', qc, kc) * jnp.exp(D - m_t[..., None])
        w_inter = jnp.exp(inter - m_t)
        num = jnp.einsum('bhts,bhsd->bhtd', s, vc) + w_inter[..., None] * jnp.einsum('bhvd,bhtd->bhtv', C, qc)
        den = jnp.sum(s, axis=-1) + w_inter * jnp.einsum('bhd,bhtd->bht', n, qc)
        h = num / jnp.maximum(jnp.abs(den), jnp.exp(-m_t))[..., None]
        b_last = b[..., -1]
        g = b_last[..., None] - b + ic
        m_new = jnp.maximum(b_last + m, jnp.max(g, axis=-1))
        wk = jnp.exp(g - m_new[..., None])
        dec = jnp.exp(b_last + m - m_new)
        C = dec[..., None, None] * C + jnp.einsum('bhs,bhsv,bhsd->bhvd', wk, vc, kc)
        n = dec[..., None] * n + jnp.einsum('bhs,bhsd->bhd', wk, kc)
        return (C, n, m_new), h

    (C, n, m), hs = lax.scan(step, (C0, n0, m0),
                             (chunks(q), chunks(k), chunks(v), chunks(log_i), chunks(log_f)))
    h = jnp.moveaxis(jnp.moveaxis(hs, 2, 3), 0, 1).reshape(Bsz, L, H, d)
    return h, C, n, m

def rwkv7_scan(r, decay, k, v, a, b, S0):
    def step(S, inp):
        rt, dt, kt, vt, at, bt = inp
        sa = jnp.einsum('bhvk,bhk->bhv', S, at)
        S = S * dt[:, :, None, :] + sa[..., None] * bt[:, :, None, :] + vt[..., None] * kt[:, :, None, :]
        return S, jnp.einsum('bhvk,bhk->bhv', S, rt)

    tm = lambda t: jnp.moveaxis(t, 1, 0)
    S, ys = lax.scan(step, S0, (tm(r), tm(decay), tm(k), tm(v), tm(a), tm(b)))
    return jnp.moveaxis(ys, 0, 1), S

def index_scores(iq, iw, ik, mask):
    s = jnp.einsum('bthd,bsd->bths', iq.astype(jnp.float32), ik.astype(jnp.float32))
    s = jax.nn.relu(s * IDX_DIM ** -0.5)
    score = jnp.einsum('bths,bth->bts', s, iw.astype(jnp.float32) * IDX_HEADS ** -0.5)
    return jnp.where(mask[None], score, -jnp.inf)

def sparse_attend(q, k_sel, v_sel, valid):
    Bsz, T, H, d = q.shape
    qg = q.reshape(Bsz, T, B_KV_HEADS, H // B_KV_HEADS, d)
    s = jnp.einsum('bthgd,btkhd->bthgk', qg, k_sel).astype(jnp.float32) * d ** -0.5
    s = jnp.where(valid[:, :, None, None, :], s, -jnp.inf)
    pr = jax.nn.softmax(s, axis=-1).astype(v_sel.dtype)
    o = jnp.einsum('bthgk,btkhd->bthgd', pr, v_sel)
    return o.reshape(Bsz, T, H, d)

def prompt_dsa(q, k, v, iq, ik, iw):
    Bsz, T = q.shape[:2]
    n_sel = min(TOPK_MAX, T // 4)
    qb_len = min(Q_BLOCK, T)
    nb = T // qb_len
    key_pos = jnp.arange(T, dtype=jnp.int32)

    def blk(args):
        qb, iqb, iwb, qpos = args
        sc = index_scores(iqb, iwb, ik, key_pos[None, :] <= qpos[:, None])
        vals, idx = lax.top_k(sc, n_sel)
        k_sel = jax.vmap(lambda kb, ib: kb[ib])(k, idx)
        v_sel = jax.vmap(lambda vb, ib: vb[ib])(v, idx)
        return sparse_attend(qb, k_sel, v_sel, jnp.isfinite(vals))

    to_blocks = lambda a: jnp.moveaxis(a.reshape(Bsz, nb, qb_len, *a.shape[2:]), 1, 0)
    out = lax.map(blk, (to_blocks(q), to_blocks(iq), to_blocks(iw), key_pos.reshape(nb, qb_len)))
    return jnp.moveaxis(out, 0, 1).reshape(q.shape)

def sample_dsa(q, k, v, iq, ik, iw, ck, cv, cik, page_table):
    DB, T = q.shape[:2]
    n_pages = page_table.shape[1]
    past = n_pages * PAGE_SIZE
    L = past + T
    n_sel = min(TOPK_MAX, L // 4)
    ik_all = jnp.concatenate([cik[page_table].reshape(DB, past, IDX_DIM).astype(ik.dtype), ik], axis=1)
    q_pos = past + jnp.arange(T, dtype=jnp.int32)
    key_pos = jnp.arange(L, dtype=jnp.int32)
    sc = index_scores(iq, iw, ik_all, key_pos[None, :] <= q_pos[:, None])
    vals, idx = lax.top_k(sc, n_sel)
    bidx = jnp.arange(DB)[:, None, None]
    phys = page_table[bidx, jnp.minimum(idx // PAGE_SIZE, n_pages - 1)]
    off = idx % PAGE_SIZE
    j = jnp.clip(idx - past, 0, T - 1)
    is_new = (idx >= past)[..., None, None]
    k_sel = jnp.where(is_new, k[bidx, j], ck[phys, off].astype(k.dtype))
    v_sel = jnp.where(is_new, v[bidx, j], cv[phys, off].astype(v.dtype))
    return sparse_attend(q, k_sel, v_sel, jnp.isfinite(vals))

def token_mixers(h, l, pos, mstate, shift0, S0, attn_fn, p):
    Bsz, T, _ = h.shape
    f32 = lambda a: a.astype(jnp.float32)
    heads = lambda a, n: a.reshape(Bsz, T, n, -1)
    proj = h @ p['w_in'][l]
    pa, pb, pc = split_cols(proj, (A_PROJ, B_PROJ, C_PROJ))

    aq, ak, av, ao, ag = split_cols(pa, A_SPLITS)
    gates = f32(ag) + f32(p['mlstm_gate_b'][l])
    log_i = gates[..., :A_HEADS]
    log_f = jax.nn.log_sigmoid(gates[..., A_HEADS:])
    C0, n0, m0 = mstate
    h_a, C, n, m = mlstm_chunkwise(f32(heads(aq, A_HEADS)), f32(heads(ak, A_HEADS)) * HEAD_DIM ** -0.5,
                                   f32(heads(av, A_HEADS)), log_i, log_f, f32(C0), f32(n0), f32(m0))
    h_a = rmsnorm(h_a, p['mlstm_norm'][l].reshape(A_HEADS, HEAD_DIM)).astype(h.dtype)
    y_a = jax.nn.sigmoid(ao) * h_a.reshape(Bsz, T, A_WIDTH)

    bq, bk, bv, biq, bik, biw = split_cols(pb, B_SPLITS)
    q = rotary(heads(bq, B_HEADS), pos)
    k = rotary(heads(bk, B_KV_HEADS), pos)
    v = heads(bv, B_KV_HEADS)
    iq = rotary(heads(biq, IDX_HEADS), pos)
    ik = rotary(bik[:, :, None, :], pos)[:, :, 0, :]
    y_b = attn_fn(q, k, v, iq, ik, biw).reshape(Bsz, T, B_WIDTH)

    prev = jnp.concatenate([shift0[:, None, :].astype(pc.dtype), pc[:, :-1]], axis=1)
    pcs = pc + p['rwkv_mu'][l] * (prev - pc)
    cr, ck, cv, cwl, cal, cgl = split_cols(f32(pcs), C_SPLITS)
    w = -jax.nn.softplus(-(p['rwkv_w0'][l] + jnp.tanh(cwl) @ p['rwkv_w2'][l])) - 0.5
    decay = jnp.exp(-jnp.exp(w))
    a = jax.nn.sigmoid(p['rwkv_a0'][l] + cal @ p['rwkv_a2'][l])
    g = jax.nn.sigmoid(cgl) @ p['rwkv_g2'][l]
    kk = heads(ck * p['rwkv_k_k'][l], C_HEADS)
    kk = kk / jnp.maximum(jnp.sqrt(jnp.sum(kk * kk, axis=-1, keepdims=True)), 1e-12)
    ck = ck * (1.0 + (a - 1.0) * p['rwkv_k_a'][l])
    rh, kh, vh, ah, dh = (heads(t, C_HEADS) for t in (cr, ck, cv, a, decay))
    yc, S = rwkv7_scan(rh, dh, kh, vh, -kk, kk * ah, f32(S0))
    mu = jnp.mean(yc, axis=-1, keepdims=True)
    var = jnp.mean(jnp.square(yc - mu), axis=-1, keepdims=True)
    yc = (yc - mu) * lax.rsqrt(var + RWKV_LN_EPS)
    yc = yc * p['rwkv_ln_w'][l].reshape(C_HEADS, HEAD_DIM) + p['rwkv_ln_b'][l].reshape(C_HEADS, HEAD_DIM)
    yc = yc + jnp.sum(rh * kh * p['rwkv_r_k'][l], axis=-1, keepdims=True) * vh
    y_c = (yc.reshape(Bsz, T, C_WIDTH) * g).astype(h.dtype)

    mixed = jnp.concatenate([y_a, y_b, y_c], axis=-1) @ p['w_out'][l]
    return mixed, (k, v, ik, C, n, m, pc[:, -1], S)

def hybrid_layer(x, l, pos, mstate, shift0, S0, attn_fn, p):
    mixed, new = token_mixers(rmsnorm(x, p['norm_mix'][l]), l, pos, mstate, shift0, S0, attn_fn, p)
    x = x + mixed
    hf = rmsnorm(x, p['norm_ffn'][l])
    x = x + (jax.nn.silu(hf @ p['w_gate'][l]) * (hf @ p['w_up'][l])) @ p['w_down'][l]
    return x, new

def setup_inputs(seed: int = 0) -> dict:
    key = jax.random.key(seed)
    ks = list(jax.random.split(key, 40))
    nrm = lambda i, shape, scale: scale * jax.random.normal(ks[i], shape, jnp.float32)
    n_pages = PAST_LEN // PAGE_SIZE
    n_pool = (5 * DEC_BATCH * n_pages) // 4
    page_table = jax.random.permutation(ks[10], n_pool)[:DEC_BATCH * n_pages]
    page_table = page_table.reshape(DEC_BATCH, n_pages).astype(jnp.int32)
    gate_b = jnp.concatenate([nrm(13, (DEPTH, A_HEADS), 0.1), 3.0 + nrm(14, (DEPTH, A_HEADS), 0.5)], axis=-1)
    return {
        'x_prompt': nrm(0, (BATCH, SEQ, D_MODEL), 1.0),
        'x_sample': nrm(1, (DEC_BATCH, DEC_SEQ, D_MODEL), 1.0),
        'cache_k': nrm(2, (DEPTH, n_pool, PAGE_SIZE, B_KV_HEADS, HEAD_DIM), 1.0),
        'cache_v': nrm(3, (DEPTH, n_pool, PAGE_SIZE, B_KV_HEADS, HEAD_DIM), 1.0),
        'cache_idx_k': nrm(4, (DEPTH, n_pool, PAGE_SIZE, IDX_DIM), 1.0),
        'state_mlstm_C': nrm(5, (DEPTH, DEC_BATCH, A_HEADS, HEAD_DIM, HEAD_DIM), 0.1),
        'state_mlstm_n': nrm(6, (DEPTH, DEC_BATCH, A_HEADS, HEAD_DIM), 1.0),
        'state_mlstm_m': nrm(7, (DEPTH, DEC_BATCH, A_HEADS), 0.5),
        'state_rwkv_shift': nrm(8, (DEPTH, DEC_BATCH, C_PROJ), 1.0),
        'state_rwkv_S': nrm(9, (DEPTH, DEC_BATCH, C_HEADS, HEAD_DIM, HEAD_DIM), 0.1),
        'page_table': page_table,
        'norm_mix': 1.0 + nrm(11, (DEPTH, D_MODEL), 0.02),
        'w_in': nrm(12, (DEPTH, D_MODEL, P_IN), D_MODEL ** -0.5),
        'mlstm_gate_b': gate_b,
        'mlstm_norm': 1.0 + nrm(15, (DEPTH, A_WIDTH), 0.02),
        'rwkv_mu': jax.random.uniform(ks[16], (DEPTH, C_PROJ), jnp.float32),
        'rwkv_w0': -2.0 + nrm(17, (DEPTH, C_WIDTH), 0.5),
        'rwkv_w2': nrm(18, (DEPTH, DECAY_LORA, C_WIDTH), 0.1 * DECAY_LORA ** -0.5),
        'rwkv_a0': nrm(19, (DEPTH, C_WIDTH), 0.1),
        'rwkv_a2': nrm(20, (DEPTH, AAA_LORA, C_WIDTH), 0.1 * AAA_LORA ** -0.5),
        'rwkv_g2': nrm(21, (DEPTH, GATE_LORA, C_WIDTH), GATE_LORA ** -0.5),
        'rwkv_k_k': 0.85 + nrm(22, (DEPTH, C_WIDTH), 0.05),
        'rwkv_k_a': 1.0 + nrm(23, (DEPTH, C_WIDTH), 0.05),
        'rwkv_r_k': nrm(24, (DEPTH, C_HEADS, HEAD_DIM), 0.1),
        'rwkv_ln_w': 1.0 + nrm(25, (DEPTH, C_WIDTH), 0.02),
        'rwkv_ln_b': nrm(26, (DEPTH, C_WIDTH), 0.01),
        'w_out': nrm(27, (DEPTH, MIX_WIDTH, D_MODEL), MIX_WIDTH ** -0.5),
        'norm_ffn': 1.0 + nrm(28, (DEPTH, D_MODEL), 0.02),
        'w_gate': nrm(29, (DEPTH, D_MODEL, D_FF), D_MODEL ** -0.5),
        'w_up': nrm(30, (DEPTH, D_MODEL, D_FF), D_MODEL ** -0.5),
        'w_down': nrm(31, (DEPTH, D_FF, D_MODEL), D_FF ** -0.5),
        'norm_final': 1.0 + nrm(32, (D_MODEL,), 0.02),
    }

def reference(x_prompt, x_sample, cache_k, cache_v, cache_idx_k, state_mlstm_C, state_mlstm_n,
              state_mlstm_m, state_rwkv_shift, state_rwkv_S, page_table, norm_mix, w_in, mlstm_gate_b,
              mlstm_norm, rwkv_mu, rwkv_w0, rwkv_w2, rwkv_a0, rwkv_a2, rwkv_g2, rwkv_k_k, rwkv_k_a,
              rwkv_r_k, rwkv_ln_w, rwkv_ln_b, w_out, norm_ffn, w_gate, w_up, w_down, norm_final):
    p = dict(norm_mix=norm_mix, w_in=w_in, mlstm_gate_b=mlstm_gate_b, mlstm_norm=mlstm_norm,
             rwkv_mu=rwkv_mu, rwkv_w0=rwkv_w0, rwkv_w2=rwkv_w2, rwkv_a0=rwkv_a0, rwkv_a2=rwkv_a2,
             rwkv_g2=rwkv_g2, rwkv_k_k=rwkv_k_k, rwkv_k_a=rwkv_k_a, rwkv_r_k=rwkv_r_k,
             rwkv_ln_w=rwkv_ln_w, rwkv_ln_b=rwkv_ln_b, w_out=w_out, norm_ffn=norm_ffn,
             w_gate=w_gate, w_up=w_up, w_down=w_down)
    Bp, Tp = x_prompt.shape[:2]
    Ts = x_sample.shape[1]
    past = page_table.shape[1] * PAGE_SIZE
    pos_p = jnp.arange(Tp, dtype=jnp.int32)
    pos_s = past + jnp.arange(Ts, dtype=jnp.int32)
    zC = jnp.zeros((Bp, A_HEADS, HEAD_DIM, HEAD_DIM), jnp.float32)
    zn = jnp.zeros((Bp, A_HEADS, HEAD_DIM), jnp.float32)
    zm = jnp.zeros((Bp, A_HEADS), jnp.float32)
    zshift = jnp.zeros((Bp, C_PROJ), x_prompt.dtype)
    zS = jnp.zeros((Bp, C_HEADS, HEAD_DIM, HEAD_DIM), jnp.float32)
    xp, xs = x_prompt, x_sample
    new_p, new_s = [], []
    for l in range(DEPTH):
        xp, st = hybrid_layer(xp, l, pos_p, (zC, zn, zm), zshift, zS, prompt_dsa, p)
        new_p.append(st)
        attn_s = functools.partial(sample_dsa, ck=cache_k[l], cv=cache_v[l], cik=cache_idx_k[l],
                                   page_table=page_table)
        xs, st = hybrid_layer(xs, l, pos_s, (state_mlstm_C[l], state_mlstm_n[l], state_mlstm_m[l]),
                              state_rwkv_shift[l], state_rwkv_S[l], attn_s, p)
        new_s.append(st)
    y_prompt = rmsnorm(xp, norm_final)
    y_sample = rmsnorm(xs, norm_final)
    stack = lambda states, i: jnp.stack([st[i] for st in states])
    p_k, p_v, p_idx_k, p_mlstm_C, p_mlstm_n, p_mlstm_m, p_rwkv_shift, p_rwkv_S = [stack(new_p, i) for i in range(8)]
    s_k, s_v, s_idx_k, s_mlstm_C, s_mlstm_n, s_mlstm_m, s_rwkv_shift, s_rwkv_S = [stack(new_s, i) for i in range(8)]
    return (y_prompt, y_sample, p_k, p_v, p_idx_k, p_mlstm_C, p_mlstm_n, p_mlstm_m, p_rwkv_shift, p_rwkv_S,
            s_k, s_v, s_idx_k, s_mlstm_C, s_mlstm_n, s_mlstm_m, s_rwkv_shift, s_rwkv_S)


_drawn_inputs = setup_inputs


def setup_inputs(seed=0):
    import zlib

    import numpy as np

    out = dict(_drawn_inputs(seed))
    spreads = {}
    factors = {'mlstm_norm': 5.364,
     'rwkv_w2': 5.337,
     'rwkv_k_k': 2.854,
     'rwkv_ln_w': 5.215,
     'rwkv_ln_b': 21.807,
     'norm_final': 7.475,
     'norm_ffn': 4.348}
    for name, (base, spread) in spreads.items():
        noise = np.random.default_rng([zlib.crc32(name.encode()), seed]).standard_normal(out[name].shape)
        drawn = base * np.exp(spread * noise) if base else spread * noise
        out[name] = jnp.asarray(drawn.astype(out[name].dtype))
    for name, factor in factors.items():
        out[name] = (out[name] * factor).astype(out[name].dtype)
    return out
```

```python
from contextlib import ExitStack
import math

import numpy as np
import concourse.bass as bass
from concourse import mybir

F32 = mybir.dt.float32
U32 = mybir.dt.uint32
I32 = mybir.dt.int32
ALU = mybir.AluOpType
ACT = mybir.ActivationFunctionType
AX = mybir.AxisListType.X

P = 128
D = 1024
KT = D // P
SEQ = 1024
DEPTH = 2
DB = 8
DT = 8
NS = DB * DT
NT = SEQ // P
TILES = NT + 1
ROWS = TILES * P
HD = 64
AH = 4
AW = 256
BW = 512
BH = 8
KVH = 4
CH = 4
CW = 256
IH = 8
TOPK = 256
PAGE = 128
NPAGES = 64
PAST = NPAGES * PAGE
HALF = PAST // 2
DFF = 2816
FT = DFF // P
A_PROJ = 4 * AW + 2 * AH
B_PROJ = BW + 2 * KVH * HD + IH * HD + HD + IH
C_PROJ = 3 * CW + 64 + 64 + 128
P_IN = A_PROJ + B_PROJ + C_PROJ
B0 = A_PROJ
C0 = A_PROJ + B_PROJ
BK0 = B0 + BW
BV0 = BK0 + KVH * HD
BIQ0 = BV0 + KVH * HD
BIK0 = BIQ0 + IH * HD
BIW0 = BIK0 + HD
EPS = 1e-6
LN_EPS = 64e-5
NEG = -1e30
CHUNK = 64


class Stage:

    def __init__(self, nc):
        self.nc = nc

    def __enter__(self):
        self.ctx = ExitStack()
        self.sems = []
        return self

    def sb(self, name, shape, dt=F32):
        return self.ctx.enter_context(self.nc.sbuf_tensor(name, shape, dt, allow_name_mangling=True))

    def ps(self, name, shape):
        return self.ctx.enter_context(self.nc.psum_tensor(name, shape, F32, allow_name_mangling=True))

    def sem(self, name):
        s = self.nc.alloc_semaphore(name=f"{name}_{self.nc.next_id()}")
        self.sems.append(s)
        return s

    def close_sems(self):
        self.nc.all_engine_barrier()
        self.nc.clear_and_free_semaphores(self.sems)
        self.nc.all_engine_barrier()
        self.sems = []

    def __exit__(self, *exc):
        if exc[0] is None and self.sems:
            self.close_sems()
        self.ctx.close()


class Chain:

    def __init__(self, eng, sem):
        self.eng, self.sem, self.n = eng, sem, 0

    def __call__(self, ins):
        self.n += 1
        ins.then_inc(self.sem, 1)
        self.eng.wait_ge(self.sem, self.n)


def rows_at(ap, r0, n=P):
    return ap[bass.ds(r0, n), :]


def layer(ap, l):
    names = " ".join(f"a{i}" for i in range(len(ap.shape) - 1))
    return ap[bass.ds(l, 1)].rearrange(f"o {names} -> (o a0) {names[3:]}") if len(ap.shape) > 2 else ap[bass.ds(l, 1), :]


def all_rows(ap, n=P):
    return ap.partition_broadcast(n)


PROJ_CHUNKS = [(0, 512), (512, 512), (1024, 8), (B0, 512), (BK0, 512), (BIQ0, 512), (BIK0, 72),
               (C0, 512), (C0 + 512, 512)]


def stage_project(nc, l, io, sc, const):
    with Stage(nc) as st:
        w = st.sb("w_in", [P, KT, P_IN])
        g = st.sb("g_mix", [P, D])
        x = st.sb("x_tile", [P, D])
        sq = st.sb("sq", [P, D])
        xT = st.sb("xT", [P, KT, P])
        pr = st.sb("proj", [P, P_IN])
        stat = st.sb("stat", [P, 4])
        cs = st.sb("cs", [P, 2, 8])
        rt = st.sb("rt", [P, 3, 12, 16])
        ikd = st.sb("ikd", [P, P])
        tT = st.sb("tT", [P, 11, P])
        pp = [st.ps(f"pp{i}", [P, 512]) for i in range(4)]
        pt = [st.ps(f"pt{i}", [P, 4, P]) for i in range(3)]

        w_loaded = st.sem("w_loaded")
        with nc.Block() as block:
            @block.sync
            def _(sp):
                for k in range(KT):
                    sp.dma_start(w[:, k, :], layer(io["w_in"], l)[k * P:(k + 1) * P, :]).then_inc(w_loaded, 16)
                sp.dma_start(g[:, :], all_rows(layer(io["norm_mix"], l)[0, :])).then_inc(w_loaded, 16)
                sp.wait_ge(w_loaded, 16 * (KT + 1))
        st.close_sems()

        with nc.Fori(0, TILES) as i:
            x_loaded = st.sem("x_loaded")
            sumsq = st.sem("sumsq")
            root = st.sem("root")
            normed = st.sem("normed")
            xT_psum = st.sem("xT_psum")
            xT_ready = st.sem("xT_ready")
            chunk_done = st.sem("chunk_done")
            chunk_out = st.sem("chunk_out")
            chain_s = st.sem("dve_chain")
            rotated = st.sem("rotated")
            turned = st.sem("turned")
            turned_out = st.sem("turned_out")
            stored = st.sem("stored")
            with nc.Block() as block:
                @block.sync
                def _(sp):
                    r = i * P
                    sp.dma_start(x[:, :], rows_at(sc["x"], r)).then_inc(x_loaded, 16)
                    sp.dma_start(cs[:, :, :].rearrange("p a b -> p (a b)"), rows_at(io["rope"], r)).then_inc(x_loaded, 16)
                    sp.wait_ge(chunk_out, 9)
                    sp.dma_start(rows_at(sc["pa"], r), pr[:, 0:A_PROJ]).then_inc(stored, 16)
                    sp.dma_start(rows_at(sc["v"], r), pr[:, BV0:BIQ0]).then_inc(stored, 16)
                    sp.dma_start(rows_at(sc["iw"], r), pr[:, BIW0:C0]).then_inc(stored, 16)
                    sp.dma_start(rows_at(sc["pc"], r), pr[:, C0:P_IN]).then_inc(stored, 16)
                    sp.dma_start(rows_at(sc["prev"], r + 1), pr[:, C0:P_IN]).then_inc(stored, 16)
                    sp.wait_ge(rotated, 1)
                    sp.dma_start(rows_at(sc["k"], r), pr[:, BK0:BV0]).then_inc(stored, 16)
                    sp.dma_start(rows_at(sc["ik"], r), pr[:, BIK0:BIW0]).then_inc(stored, 16)
                    sp.wait_ge(turned_out, 3)
                    for j in range(4):
                        sp.dma_start(sc["qT"][j, :, bass.ds(r, P)], tT[:, j, :]).then_inc(stored, 16)
                        sp.dma_start(sc["iqT"][j, :, bass.ds(r, P)], tT[:, 6 + j, :]).then_inc(stored, 16)
                    for j in range(2):
                        sp.dma_start(sc["kT"][j, :, bass.ds(r, P)], tT[:, 4 + j, :]).then_inc(stored, 16)
                    sp.dma_start(sc["ikT"][:, bass.ds(r, P)], tT[:, 10, :]).then_inc(stored, 16)
                    sp.wait_ge(stored, 16 * 18)

                @block.scalar
                def _(act):
                    act.wait_ge(x_loaded, 32)
                    act.activation(sq[:, :], x[:, :], ACT.Square, accum_out=stat[:, 0:1]).then_inc(sumsq, 1)
                    act.wait_ge(sumsq, 1)
                    act.activation(stat[:, 1:2], stat[:, 0:1], ACT.Sqrt, bias=const["eps"][:, 0:1], scale=1.0 / D).then_inc(root, 1)
                    for n, (c0, cw) in enumerate(PROJ_CHUNKS):
                        act.wait_ge(chunk_done, n + 1)
                        act.activation(pr[:, c0:c0 + cw], pp[n % 4][:, 0:cw], ACT.Copy).then_inc(chunk_out, 1)

                @block.vector
                def _(dve):
                    chain = Chain(dve, chain_s)
                    dve.wait_ge(root, 1)
                    chain(dve.reciprocal(stat[:, 2:3], stat[:, 1:2]))
                    dve.scalar_tensor_tensor(out=sq[:, :], in0=x[:, :], scalar=stat[:, 2:3], in1=g[:, :],
                                             op0=ALU.mult, op1=ALU.mult).then_inc(normed, 1)
                    for n in range(2):
                        dve.wait_ge(xT_psum, n + 1)
                        dve.tensor_copy(xT[:, 4 * n:4 * n + 4, :], pt[n][:, :, :]).then_inc(xT_ready, 1)
                    dve.wait_ge(chunk_out, 7)
                    for c0, nh in ((B0, 12), (BIQ0, 9)):
                        v = pr[:, c0:c0 + nh * HD].rearrange("p (h d) -> p h d", d=HD)
                        cos = cs[:, 0:1, :].to_broadcast([P, nh, 8])
                        sin = cs[:, 1:2, :].to_broadcast([P, nh, 8])
                        a, b = v[:, :, 0:8], v[:, :, 8:16]
                        t = [rt[:, k, 0:nh, :] for k in range(3)]
                        dve.tensor_tensor(t[0][:, :, 0:8], a, cos, ALU.mult)
                        dve.tensor_tensor(t[0][:, :, 8:16], b, cos, ALU.mult)
                        dve.tensor_tensor(t[1][:, :, 0:8], b, sin, ALU.mult)
                        chain(dve.tensor_tensor(t[1][:, :, 8:16], a, sin, ALU.mult))
                        dve.tensor_tensor(a, t[0][:, :, 0:8], t[1][:, :, 0:8], ALU.subtract)
                        chain(dve.tensor_tensor(b, t[0][:, :, 8:16], t[1][:, :, 8:16], ALU.add))
                    q = pr[:, B0:BK0].rearrange("p (a e g d) -> p a g e d", a=2, e=2, g=2)
                    qo = sq[:, 0:BW].rearrange("p (a g e d) -> p a g e d", a=2, g=2, e=2)
                    for a in range(2):
                        dve.tensor_copy(qo[:, a], q[:, a])
                    dve.tensor_copy(ikd[:, 0:HD], pr[:, BIK0:BIW0])
                    dve.tensor_copy(ikd[:, HD:P], pr[:, BIK0:BIW0]).then_inc(rotated, 1)
                    for n in range(3):
                        dve.wait_ge(turned, n + 1)
                        m = min(4, 11 - 4 * n)
                        dve.tensor_copy(tT[:, 4 * n:4 * n + m, :], pt[n][:, 0:m, :]).then_inc(turned_out, 1)

                @block.tensor
                def _(pe):
                    ident = const["ident"][:, :]
                    pe.wait_ge(normed, 1)
                    for k in range(KT):
                        ins = pe.transpose(pt[k // 4][:, k % 4, :], sq[:, k * P:(k + 1) * P], ident)
                        if k % 4 == 3:
                            ins.then_inc(xT_psum, 1)
                    pe.wait_ge(xT_ready, 2)
                    for n, (c0, cw) in enumerate(PROJ_CHUNKS):
                        if n >= 4:
                            pe.wait_ge(chunk_out, n - 3)
                        for k in range(KT):
                            ins = pe.matmul(pp[n % 4][:, 0:cw], xT[:, k, :], w[:, k, c0:c0 + cw],
                                            start=(k == 0), stop=(k == KT - 1))
                        ins.then_inc(chunk_done, 1)
                    pe.wait_ge(rotated, 1)
                    srcs = [sq[:, j * P:(j + 1) * P] for j in range(4)]
                    srcs += [pr[:, BK0 + j * P:BK0 + (j + 1) * P] for j in range(2)]
                    srcs += [pr[:, BIQ0 + j * P:BIQ0 + (j + 1) * P] for j in range(4)]
                    srcs += [ikd[:, :]]
                    for n, s in enumerate(srcs):
                        ins = pe.transpose(pt[n // 4][:, n % 4, :], s, ident)
                        if n % 4 == 3 or n == 10:
                            ins.then_inc(turned, 1)
            st.close_sems()

        fixed = st.sem("fixed")
        with nc.Block() as block:
            @block.sync
            def _(sp):
                sp.dma_start(sc["prev"][0:1, :], const["zeros"][0:1, 0:D]).then_inc(fixed, 16)
                sp.dma_start(sc["prev"][SEQ:SEQ + NS, :].rearrange("(b t) n -> b t n", t=DT)[:, 0, :],
                             layer(io["state_rwkv_shift"], l)).then_inc(fixed, 16)
                S = SEQ
                n = 2
                for name, k in (("k", "k"), ("v", "v"), ("idx_k", "ik")):
                    flat = "o b t h d -> (o b t) (h d)" if name != "idx_k" else "o b t d -> (o b t) d"
                    sp.dma_start(io["p_" + name][bass.ds(l, 1)].rearrange(flat), sc[k][0:S, :]).then_inc(fixed, 16)
                    sp.dma_start(io["s_" + name][bass.ds(l, 1)].rearrange(flat), sc[k][S:S + NS, :]).then_inc(fixed, 16)
                    n += 2
                sp.dma_start(io["p_rwkv_shift"][bass.ds(l, 1)].rearrange("o b n -> (o b) n"), sc["pc"][S - 1:S, :]).then_inc(fixed, 16)
                sp.dma_start(io["s_rwkv_shift"][bass.ds(l, 1)].rearrange("o b n -> (o b) n"),
                             sc["pc"][S:S + NS, :].rearrange("(b t) n -> b t n", t=DT)[:, DT - 1, :]).then_inc(fixed, 16)
                sp.wait_ge(fixed, 16 * (n + 2))


def stage_mlstm(nc, l, io, sc, const):
    H1 = HD + 1

    def group(seqs, W, tiles, row0, tag):
        G, L = seqs, W // seqs
        with Stage(nc) as st:
            gb = st.sb("gate_bias", [P, 2 * AH])
            nw = st.sb("norm_w", [P, AW])
            sel = st.sb("sel", [AH, AH, P])
            CT = st.sb("CT", [HD, AH, G, H1])
            mp = st.sb("m_prev", [AH, G])
            a = st.sb("a_tile", [P, A_PROJ])
            gt = st.sb("gates", [P, 2 * AH])
            fr = st.sb("f_rows", [AH, 4, W])
            ir = st.sb("i_rows", [AH, W])
            b = st.sb("b_rows", [AH, W])
            m = st.sb("m_rows", [AH, W])
            bml = st.sb("bml", [AH, G])
            dec = st.sb("dec", [AH, G])
            dg = st.sb("dec_diag", [AH, AH, G])
            decb = st.sb("dec_b", [HD, AH, G])
            r = st.sb("rows", [AH, 4, W])
            er = st.sb("exp_rows", [AH, 3, W])
            col = st.sb("cols", [P, 4, AH])
            u = st.sb("u_rows", [AH, W])
            E = st.sb("decay", [P, AH, W])
            S = st.sb("scores", [P, AH, W])
            qk = st.sb("qkT", [HD, 8, W])
            v1 = st.sb("v1", [P, AH, H1])
            kw = st.sb("kw", [P, AH, HD])
            t1 = st.sb("inter", [P, AH, H1])
            nd = st.sb("num_den", [P, AH, H1])
            dn = st.sb("den", [P, 4, AH])
            h = st.sb("h", [P, AH, HD])
            hs = st.sb("h_sq", [P, AH, HD])
            og = st.sb("out_gate", [P, 2, AW])
            nat = st.sb("C_natural", [HD, G, AH, HD])
            nn = st.sb("n_natural", [G, AW])
            if G > 1:
                qm = st.sb("q_masked", [HD, AH, G, W])
                vm = st.sb("v_masked", [P, AH, G, H1])
            psm = st.ps("p_small", [P, 512])
            pg = psm[0:AH, 0:2 * W].rearrange("p (a t) -> p a t", a=2)
            pc = psm[:, 256:256 + 4 * AH].rearrange("p (a h) -> p a h", h=AH)
            pd = psm[0:HD, 320:320 + AH * G].rearrange("p (h g) -> p h g", g=G)
            pU = st.ps("p_decay", [P, 512])
            pS = st.ps("p_scores", [P, 512])
            pq = st.ps("p_qk", [HD, 8, P])
            pN = st.ps("p_intra", [P, 512])
            pI = st.ps("p_inter", [P, 512])
            pC = [pU, pS, pN, pI]
            ident = const["ident"]

            loaded = st.sem("loaded")
            turned = st.sem("turned")
            copied = st.sem("copied")
            made = st.sem("made")
            with nc.Block() as block:
                @block.sync
                def _(sp):
                    with nc.allow_non_contiguous_dma(reason="a few state words"):
                        sp.dma_start(gb[:, :], all_rows(layer(io["mlstm_gate_b"], l)[0, :])).then_inc(loaded, 16)
                        sp.dma_start(nw[:, :], all_rows(layer(io["mlstm_norm"], l)[0, :])).then_inc(loaded, 16)
                        if G > 1:
                            sp.dma_start(mp[:, :], layer(io["state_mlstm_m"], l).rearrange("b h -> h b")).then_inc(loaded, 16)
                            sp.dma_start(nn[:, :], layer(io["state_mlstm_n"], l).rearrange("b h k -> b (h k)")).then_inc(loaded, 16)
                            for bb in range(G):
                                sp.dma_start(nat[:, bb], layer(io["state_mlstm_C"], l)[bb].rearrange("h v k -> v h k")).then_inc(loaded, 16)
                    sp.wait_ge(loaded, 32 if G == 1 else 64 + 16 * G)

                @block.vector
                def _(dve):
                    dve.memset(v1[:, :, :], 1.0).then_inc(made, 1)
                    dve.tensor_copy(sel[:, :, :], ident[0:AH, 0:AH].unsqueeze(2).to_broadcast([AH, AH, P])).then_inc(made, 1)
                    if G == 1:
                        dve.memset(CT[:, :, :, :], 0.0).then_inc(made, 1)
                        dve.memset(mp[:, :], 0.0).then_inc(made, 1)
                    else:
                        dve.memset(qm[:, :, :, :], 0.0).then_inc(made, 1)
                        for bb in range(G):
                            dve.wait_ge(turned, bb + 1)
                            dve.tensor_copy(CT[:, :, bb, 0:HD], pC[bb % 2][0:HD, 0:AH * HD].rearrange("p (a v) -> p a v", a=AH)).then_inc(copied, 1)
                        dve.wait_ge(turned, G + 1)
                        dve.tensor_copy(CT[:, :, :, HD], pq[:, 0:4, 0:G]).then_inc(copied, 1)

                @block.tensor
                def _(pe):
                    if G > 1:
                        pe.wait_ge(loaded, 64 + 16 * G)
                        for bb in range(G):
                            if bb >= 2:
                                pe.wait_ge(copied, bb - 1)
                            for k in range(AH):
                                ins = pe.transpose(pC[bb % 2][0:HD, k * HD:(k + 1) * HD], nat[:, bb, k, :], ident[0:HD, 0:HD])
                            ins.then_inc(turned, 1)
                        for k in range(AH):
                            ins = pe.transpose(pq[:, k, 0:G], nn[:, k * HD:(k + 1) * HD], ident[0:G, 0:G])
                        ins.then_inc(turned, 1)
            st.close_sems()

            def body(i):
                S_ = st.sem
                a_loaded, gates, gates_T, absd, exped = S_("a_loaded"), S_("gates"), S_("gates_T"), S_("absd"), S_("exped")
                logged, rows_s, rows_e, cols_p, dd, dec_p = S_("logged"), S_("rows"), S_("rows_exp"), S_("cols_psum"), S_("dec_diag"), S_("dec_psum")
                cols_r, qk_p, qk_r, u_r, u_p = S_("cols_ready"), S_("qk_psum"), S_("qk_ready"), S_("u_ready"), S_("u_psum")
                E_r, s_p, s_r, v_r, in_p, it_p = S_("decay_ready"), S_("s_psum"), S_("s_ready"), S_("v_ready"), S_("intra"), S_("inter")
                kw_r, st_p, chain_s, ms_r, rt_r, og_e, y_r, stored = S_("kw_ready"), S_("state_psum"), S_("dve_chain"), S_("ms"), S_("root"), S_("og_exp"), S_("y_ready"), S_("stored")
                qm_r, nd_r, st_r = S_("qm_ready"), S_("nd_ready"), S_("state_ready")

                with nc.Block() as block:
                    @block.sync
                    def _(sp):
                        rr = i * P + row0
                        sp.dma_start(a[:, :], rows_at(sc["pa"], rr)).then_inc(a_loaded, 16)
                        sp.wait_ge(y_r, 1)
                        sp.dma_start(sc["y"][bass.ds(rr, W), 0:AW], og[0:W, 1, :]).then_inc(stored, 16)
                        sp.wait_ge(stored, 16)

                    @block.tensor
                    def _(pe):
                        pe.wait_ge(a_loaded, 16)
                        for n in range(8):
                            ins = pe.transpose(pq[:, n, 0:W], a[0:W, n * HD:(n + 1) * HD], ident[0:W, 0:W])
                        ins.then_inc(qk_p, 1)
                        pe.wait_ge(gates, 1)
                        for n in range(2):
                            ins = pe.transpose(pg[:, n, :], gt[0:W, n * AH:(n + 1) * AH], ident[0:W, 0:W])
                        ins.then_inc(gates_T, 1)
                        pe.wait_ge(qk_r, 1)
                        for hh in range(AH):
                            ins = pe.matmul(pS[0:W, hh * W:(hh + 1) * W], qk[:, AH + hh, :], qk[:, hh, :], start=True, stop=True)
                        ins.then_inc(s_p, 1)
                        pe.wait_ge(rows_s, 1)
                        mask = const["masks"][0:W, CAUSAL_ST if G == 1 else CAUSAL_ST8, 0:W]
                        for hh in range(AH):
                            pe.matmul(pU[0:W, hh * W:(hh + 1) * W], sel[:, hh, 0:W], u[:, :], start=True, stop=False)
                            ins = pe.matmul(pU[0:W, hh * W:(hh + 1) * W], ident[0:W, 0:W], mask, start=False, stop=True)
                        ins.then_inc(u_p, 1)
                        if G > 1:
                            pe.wait_ge(qm_r, AH)
                        for hh in range(AH):
                            for bb in range(G):
                                q = qk[:, hh, :] if G == 1 else qm[:, hh, bb, :]
                                ins = pe.matmul(pI[0:W, hh * H1:(hh + 1) * H1], q, CT[:, hh, bb, :], start=(bb == 0), stop=(bb == G - 1))
                        ins.then_inc(it_p, 1)
                        pe.wait_ge(rows_e, 1)
                        for n in range(4):
                            ins = pe.transpose(pc[0:W, n, :], r[:, 0, :] if n == 0 else er[:, n - 1, :], ident[0:AH, 0:AH])
                        ins.then_inc(cols_p, 1)
                        pe.wait_ge(dd, 1)
                        pe.wait_ge(cols_r, 1)
                        pe.matmul(pd, const["ones"][0:AH, 0:HD], dg[:, :, :], start=True, stop=True).then_inc(dec_p, 1)
                        pe.wait_ge(s_r, 1)
                        pe.wait_ge(v_r, 1)
                        for hh in range(AH):
                            ins = pe.matmul(pN[0:W, hh * H1:(hh + 1) * H1], S[0:W, hh, :], v1[0:W, hh, :], start=True, stop=True)
                        ins.then_inc(in_p, 1)
                        pe.wait_ge(kw_r, 1)
                        pe.wait_ge(E_r, AH)
                        pe.wait_ge(nd_r, 1)
                        for hh in range(AH):
                            if G == 1:
                                ins = pe.matmul(pC[0][0:HD, hh * H1:hh * H1 + H1], kw[0:W, hh, :], v1[0:W, hh, :], start=True, stop=True)
                            else:
                                if hh >= 2:
                                    pe.wait_ge(st_r, hh - 1)
                                for g2 in range(2):
                                    ins = pe.matmul(pC[hh % 2 * 2 + g2][0:HD, 0:4 * H1], kw[0:W, hh, :], vm[0:W, hh, 4 * g2:4 * g2 + 4, :],
                                                    start=True, stop=True)
                                if hh < AH - 1:
                                    ins.then_inc(st_p, 1)
                        ins.then_inc(st_p, 1)

                    @block.scalar
                    def _(act):
                        act.wait_ge(qk_p, 1)
                        act.activation(qk[:, :, :], pq[:, :, 0:W], ACT.Copy).then_inc(qk_r, 1)
                        act.activation(og[0:W, 0, :], a[0:W, 3 * AW:4 * AW], ACT.Exp, scale=-1.0).then_inc(og_e, 1)
                        act.wait_ge(absd, 1)
                        act.activation(fr[:, 1, :], fr[:, 0, :], ACT.Exp, scale=-1.0).then_inc(exped, 1)
                        act.wait_ge(exped, 1)
                        act.activation(fr[:, 2, :], fr[:, 1, :], ACT.Ln, bias=const["ones"][0:AH, 0:1]).then_inc(logged, 1)
                        act.wait_ge(rows_s, 1)
                        act.activation(dec[:, :], bml[:, :], ACT.Exp)
                        act.activation(er[:, :, :], r[:, 1:4, :], ACT.Exp).then_inc(rows_e, 1)
                        act.wait_ge(cols_r, 1)
                        act.wait_ge(u_p, 1)
                        for hh in range(AH):
                            act.activation(E[0:W, hh, :], pU[0:W, hh * W:(hh + 1) * W], ACT.Exp, bias=col[0:W, 0, hh:hh + 1]).then_inc(E_r, 1)
                        act.wait_ge(ms_r, 1)
                        act.activation(dn[0:W, 2, :], dn[0:W, 1, :], ACT.Sqrt, bias=const["eps"][0:W, 0:1], scale=1.0 / HD).then_inc(rt_r, 1)

                    @block.vector
                    def _(dve):
                        chain = Chain(dve, chain_s)
                        dve.wait_ge(a_loaded, 16)
                        dve.tensor_tensor(gt[:, :], a[:, 4 * AW:A_PROJ], gb[:, :], ALU.add).then_inc(gates, 1)
                        dve.tensor_copy(v1[:, :, 0:HD], a[:, 2 * AW:3 * AW].rearrange("p (h d) -> p h d", d=HD)).then_inc(v_r, 1)
                        if G > 1:
                            dve.wait_ge(qk_r, 1)
                            for k in range(AH):
                                for bb in range(G):
                                    ins = dve.tensor_copy(qm[:, k, bb, bb * L:(bb + 1) * L], qk[:, k, bb * L:(bb + 1) * L])
                                ins.then_inc(qm_r, 1)
                            dve.wait_ge(v_r, 1)
                            for hh in range(AH):
                                dve.tensor_tensor(vm[0:W, hh, :, :], v1[0:W, hh, :].unsqueeze(1).to_broadcast([W, G, H1]),
                                                  const["masks"][0:W, SEQ_OF, 0:G].unsqueeze(2).to_broadcast([W, G, H1]), ALU.mult)
                        dve.wait_ge(gates_T, 1)
                        dve.tensor_copy(ir[:, :], pg[:, 0, :])
                        chain(dve.tensor_copy(fr[:, 3, :], pg[:, 1, :]))
                        chain(dve.scalar_tensor_tensor(out=fr[:, 0, :], in0=fr[:, 3, :], scalar=-1.0, in1=fr[:, 3, :], op0=ALU.mult, op1=ALU.max))
                        dve.tensor_scalar(fr[:, 3, :], fr[:, 3, :], 0.0, None, ALU.min).then_inc(absd, 1)
                        dve.wait_ge(absd, 1)
                        dve.wait_ge(logged, 1)
                        chain(dve.tensor_tensor(fr[:, 3, :], fr[:, 3, :], fr[:, 2, :], ALU.subtract))
                        for bb in range(G):
                            s = slice(bb * L, (bb + 1) * L)
                            dve.tensor_tensor_scan(b[:, s], const["ones"][0:AH, 0:L], fr[:, 3, s], 0.0, ALU.mult, ALU.add)
                            last = dve.tensor_tensor_scan(m[:, s], fr[:, 3, s], ir[:, s], mp[:, bb:bb + 1], ALU.add, ALU.max)
                        chain(last)
                        seq = lambda t: t.rearrange("p (g t) -> p g t", g=G)
                        dve.tensor_tensor(r[:, 0, :], ir[:, :], b[:, :], ALU.subtract)
                        dve.tensor_tensor(u[:, :], b[:, :], m[:, :], ALU.subtract)
                        dve.tensor_scalar(r[:, 3, :], m[:, :], -1.0, None, ALU.mult)
                        chain(dve.tensor_tensor(bml[:, :], seq(b[:, :])[:, :, L - 1], seq(m[:, :])[:, :, L - 1], ALU.subtract))
                        dve.tensor_tensor(seq(r[:, 1, :]), seq(r[:, 0, :]), bml[:, :].unsqueeze(2).to_broadcast([AH, G, L]), ALU.add)
                        chain(dve.tensor_tensor(seq(r[:, 2, :]), seq(u[:, :]), mp[:, :].unsqueeze(2).to_broadcast([AH, G, L]), ALU.add))
                        chain(dve.tensor_tensor(bml[:, :], bml[:, :], mp[:, :], ALU.add))
                        dve.tensor_copy(mp[:, :], seq(m[:, :])[:, :, L - 1]).then_inc(rows_s, 1)
                        dve.wait_ge(rows_e, 1)
                        dve.tensor_tensor(dg[:, :, :], ident[0:AH, 0:AH].unsqueeze(2).to_broadcast([AH, AH, G]),
                                          dec[:, :].unsqueeze(1).to_broadcast([AH, AH, G]), ALU.mult).then_inc(dd, 1)
                        dve.wait_ge(cols_p, 1)
                        dve.tensor_copy(col[0:W, :, :], pc[0:W, :, :]).then_inc(cols_r, 1)
                        dve.wait_ge(dec_p, 1)
                        chain(dve.tensor_copy(decb[:, :, :], pd))
                        dve.wait_ge(cols_r, 1)
                        dve.scalar_tensor_tensor(out=kw[0:W, :, :], in0=a[0:W, AW:2 * AW].rearrange("p (h d) -> p h d", d=HD), scalar=HD ** -0.5,
                                                 in1=col[0:W, 1, :].unsqueeze(2).to_broadcast([W, AH, HD]), op0=ALU.mult, op1=ALU.mult).then_inc(kw_r, 1)
                        dve.wait_ge(E_r, AH)
                        dve.wait_ge(s_p, 1)
                        dve.scalar_tensor_tensor(out=S[0:W, :, :].rearrange("p h t -> p (h t)"), in0=pS[0:W, 0:AH * W], scalar=HD ** -0.5,
                                                 in1=E[0:W, :, :].rearrange("p h t -> p (h t)"), op0=ALU.mult, op1=ALU.mult).then_inc(s_r, 1)
                        dve.wait_ge(it_p, 1)
                        chain(dve.tensor_tensor(t1[0:W, :, :], pI[0:W, 0:AH * H1].rearrange("p (h v) -> p h v", v=H1),
                                                col[0:W, 2, :].unsqueeze(2).to_broadcast([W, AH, H1]), ALU.mult))
                        dve.wait_ge(in_p, 1)
                        ins = dve.tensor_tensor(nd[0:W, :, :], pN[0:W, 0:AH * H1].rearrange("p (h v) -> p h v", v=H1), t1[0:W, :, :], ALU.add)
                        ins.then_inc(nd_r, 1)
                        dve.wait_ge(nd_r, 1)
                        chain(dve.scalar_tensor_tensor(out=dn[0:W, 0, :], in0=nd[0:W, :, HD], scalar=-1.0, in1=nd[0:W, :, HD], op0=ALU.mult, op1=ALU.max))
                        chain(dve.tensor_tensor(dn[0:W, 0, :], dn[0:W, 0, :], col[0:W, 3, :], ALU.max))
                        chain(dve.reciprocal(dn[0:W, 1, :], dn[0:W, 0, :]))
                        chain(dve.tensor_tensor(h[0:W, :, :], nd[0:W, :, 0:HD], dn[0:W, 1, :].unsqueeze(2).to_broadcast([W, AH, HD]), ALU.mult))
                        chain(dve.tensor_tensor(hs[0:W, :, :], h[0:W, :, :], h[0:W, :, :], ALU.mult))
                        dve.tensor_reduce(dn[0:W, 1, :], hs[0:W, :, :], AX, ALU.add).then_inc(ms_r, 1)
                        chain(dve.tensor_tensor(CT[:, :, :, :], CT[:, :, :, :], decb[:, :, :].unsqueeze(3).to_broadcast([HD, AH, G, H1]), ALU.mult))
                        if G == 1:
                            dve.wait_ge(st_p, 1)
                            chain(dve.tensor_tensor(CT[:, :, 0, :], pC[0][0:HD, 0:AH * H1].rearrange("p (a v) -> p a v", v=H1), CT[:, :, 0, :], ALU.add))
                        else:
                            for k in range(AH):
                                dve.wait_ge(st_p, k + 1)
                                for g2 in range(2):
                                    ins = dve.tensor_tensor(CT[:, k, 4 * g2:4 * g2 + 4, :], pC[k % 2 * 2 + g2][0:HD, 0:4 * H1].rearrange("p (g v) -> p g v", v=H1),
                                                            CT[:, k, 4 * g2:4 * g2 + 4, :], ALU.add)
                                ins.then_inc(st_r, 1)
                        dve.wait_ge(og_e, 1)
                        chain(dve.tensor_scalar(og[0:W, 0, :], og[0:W, 0, :], 1.0, None, ALU.add))
                        chain(dve.reciprocal(og[0:W, 1, :], og[0:W, 0, :]))
                        chain(dve.tensor_tensor(og[0:W, 1, :], og[0:W, 1, :], nw[0:W, :], ALU.mult))
                        dve.wait_ge(rt_r, 1)
                        chain(dve.reciprocal(dn[0:W, 3, :], dn[0:W, 2, :]))
                        chain(dve.tensor_tensor(h[0:W, :, :], h[0:W, :, :], dn[0:W, 3, :].unsqueeze(2).to_broadcast([W, AH, HD]), ALU.mult))
                        dve.tensor_tensor(og[0:W, 1, :], og[0:W, 1, :], h[0:W, :, :].rearrange("p h d -> p (h d)"), ALU.mult).then_inc(y_r, 1)
                st.close_sems()

            if tiles > 1:
                with nc.Fori(0, tiles) as i:
                    body(i)
            else:
                body(0)

            turned = st.sem("turned")
            copied = st.sem("copied")
            stored = st.sem("stored")
            with nc.Block() as block:
                @block.tensor
                def _(pe):
                    for bb in range(G):
                        if bb >= 2:
                            pe.wait_ge(copied, bb - 1)
                        for k in range(AH):
                            ins = pe.transpose(pC[bb % 2][0:HD, k * HD:(k + 1) * HD], CT[:, k, bb, 0:HD], ident[0:HD, 0:HD])
                        ins.then_inc(turned, 1)
                    for k in range(AH):
                        ins = pe.transpose(pq[0:G, k, 0:HD], CT[:, k, :, HD], ident[0:HD, 0:HD])
                    ins.then_inc(turned, 1)

                @block.vector
                def _(dve):
                    for bb in range(G):
                        dve.wait_ge(turned, bb + 1)
                        dve.tensor_copy(nat[:, bb, :, :].rearrange("p h k -> p (h k)"), pC[bb % 2][0:HD, 0:2 * P]).then_inc(copied, 1)
                    dve.wait_ge(turned, G + 1)
                    dve.tensor_copy(nn[:, :].rearrange("p (a k) -> p a k", k=HD), pq[0:G, 0:4, 0:HD]).then_inc(copied, 1)

                @block.sync
                def _(sp):
                    sp.wait_ge(copied, G + 1)
                    for bb in range(G):
                        sp.dma_start(layer(io[tag + "_mlstm_C"], l)[bb].rearrange("h v k -> v h k"), nat[:, bb]).then_inc(stored, 16)
                    sp.dma_start(layer(io[tag + "_mlstm_n"], l).rearrange("b h k -> b (h k)"), nn[:, :]).then_inc(stored, 16)
                    with nc.allow_non_contiguous_dma(reason="a few state words"):
                        sp.dma_start(layer(io[tag + "_mlstm_m"], l).rearrange("b h -> h b"), mp[:, :]).then_inc(stored, 16)
                    sp.wait_ge(stored, 16 * (G + 2))

    group(1, P, NT, 0, "p")
    group(DB, NS, 1, SEQ, "s")


def stage_rwkv(nc, l, io, sc, const):
    def group(seqs, W, tiles, row0, tag):
        G = seqs
        C = CHUNK if G == 1 else DT
        NC = W // C
        NG = 1 if G == 1 else G
        levels = int(math.log2(C))
        m_strict, m_incl = (STRICT64, INCL64) if G == 1 else (STRICT8, INCL8)
        with Stage(nc) as st:
            vec = {}
            for name, n in (("mu", C_PROJ), ("wa0", 2 * CW), ("k_k", CW), ("k_a", CW), ("r_k", CW), ("ln_w", CW), ("ln_b", CW)):
                vec[name] = st.sb("v_" + name, [P, n])
            wa2 = st.sb("wa2", [P, 2 * CW])
            g2 = st.sb("g2", [P, CW])
            ST = st.sb("ST", [HD, CH, NG, HD])
            nat = st.sb("S_natural", [HD, NG, CH, HD])
            x = st.sb("pc_tile", [P, C_PROJ])
            pv = st.sb("prev_tile", [P, C_PROJ])
            dl = st.sb("delta", [P, C_PROJ])
            lg = st.sb("lora_in", [P, 2, P])
            lT = st.sb("lora_T", [P, 2, W])
            sg = st.sb("sig", [P, 2, CW])
            zz = st.sb("z", [P, 2 * CW])
            ld = st.sb("log_decay", [P, CW])
            gg = st.sb("g_gate", [P, CW])
            ex = st.sb("expo", [P, 3, CW])
            ce = st.sb("cum_excl", [P, CW])
            dc = st.sb("chunk_decay", [HD, CH, NC])
            kk = st.sb("kk", [P, CW])
            tt = st.sb("tmp", [P, CW])
            ck = st.sb("k_new", [P, CW])
            sm = st.sb("small", [P, 10, CH])
            bon = st.sb("bonus", [P, CH])
            til = st.sb("tilde", [P, 4, CW])
            tT = st.sb("tilde_T", [HD, 4, CH, W])
            LT = st.sb("LT", [P, CH, W])
            MT = st.sb("M_T", [P, 3, CH, W])
            X = st.sb("X", [P, CH, W])
            XT = st.sb("XT", [P, CH, W])
            Y = st.sb("Yl", [P, CH, W])
            Mn = st.sb("Mn", [P, CH, W])
            U = st.sb("U", [P, CH, HD])
            Wv = st.sb("Wv", [P, CH, HD])
            GT = st.sb("GT", [HD, CH, W])
            sa = st.sb("sa", [P, CH, HD])
            y = st.sb("y", [P, CH, HD])
            yq = st.sb("y_sq", [P, CH, HD])
            if G > 1:
                gm = st.sb("GT_masked", [HD, 2, CH, NG, W])
                sm_v = st.sb("sa_v_masked", [P, 2, CH, NG, HD])
            bk = [st.ps(f"bank{n}", [P, 512]) for n in range(8)]
            ident = const["ident"]
            masks = const["masks"]

            def hw(t, W_=W):
                return t[0:W_, 0:CH * W].rearrange("p (h t) -> p h t", h=CH)

            def hv(t, n=W):
                return t[0:n, 0:CH * HD].rearrange("p (h v) -> p h v", h=CH)

            def mask4(k):
                return masks[0:W, k:k + 1, 0:W].to_broadcast([W, CH, W])

            loaded = st.sem("loaded")
            zeroed = st.sem("zeroed")
            turned = st.sem("turned")
            copied = st.sem("copied")
            with nc.Block() as block:
                @block.sync
                def _(sp):
                    one = lambda n: layer(io[n], l)[0, :] if len(io[n].shape) == 2 else layer(io[n], l).rearrange("a b -> (a b)")
                    for dst, src in ((vec["mu"][:, :], "rwkv_mu"), (vec["wa0"][:, 0:CW], "rwkv_w0"), (vec["wa0"][:, CW:2 * CW], "rwkv_a0"),
                                     (vec["k_k"][:, :], "rwkv_k_k"), (vec["k_a"][:, :], "rwkv_k_a"), (vec["r_k"][:, :], "rwkv_r_k"),
                                     (vec["ln_w"][:, :], "rwkv_ln_w"), (vec["ln_b"][:, :], "rwkv_ln_b")):
                        sp.dma_start(dst, all_rows(one(src))).then_inc(loaded, 16)
                    sp.dma_start(g2[:, :], layer(io["rwkv_g2"], l)).then_inc(loaded, 16)
                    for bb in range(G if G > 1 else 0):
                        sp.dma_start(nat[:, bb], layer(io["state_rwkv_S"], l)[bb].rearrange("h v k -> v h k")).then_inc(loaded, 16)
                    sp.wait_ge(zeroed, 1)
                    sp.dma_start(wa2[0:HD, 0:CW], layer(io["rwkv_w2"], l)).then_inc(loaded, 16)
                    sp.dma_start(wa2[HD:P, CW:2 * CW], layer(io["rwkv_a2"], l)).then_inc(loaded, 16)
                    sp.wait_ge(loaded, 16 * (11 + (G if G > 1 else 0)))

                @block.vector
                def _(dve):
                    dve.memset(wa2[:, :], 0.0).then_inc(zeroed, 1)
                    if G == 1:
                        dve.memset(ST[:, :, :, :], 0.0).then_inc(copied, 1)
                    else:
                        dve.memset(gm[:, :, :, :, :], 0.0).then_inc(copied, 1)
                        for bb in range(G):
                            dve.wait_ge(turned, bb + 1)
                            dve.tensor_copy(ST[:, :, bb, :], hv(bk[bb % 2], HD)).then_inc(copied, 1)

                @block.tensor
                def _(pe):
                    if G > 1:
                        pe.wait_ge(loaded, 16 * (11 + G))
                        for bb in range(G):
                            if bb >= 2:
                                pe.wait_ge(copied, bb)
                            for k in range(CH):
                                ins = pe.transpose(bk[bb % 2][0:HD, k * HD:(k + 1) * HD], nat[:, bb, k, :], ident[0:HD, 0:HD])
                            ins.then_inc(turned, 1)
            st.close_sems()

            def body(i):
                S_ = st.sem
                x_loaded, shifted, lora_in, lora_p, lora_T, lora_o, g_out = (S_(n) for n in ("x_loaded", "shifted", "lora_in", "lora_T_psum", "lora_T", "lora_out", "g_out"))
                z_r, sig_r, ld_r, cum_p, ce_r, exp_r, dc_p, dc_r = (S_(n) for n in ("z_ready", "sig_ready", "ld_ready", "cum_psum", "cum_excl", "exp_ready", "dc_psum", "dc_ready"))
                ss_r, nrm_r, til_r, tT_p, tT_r, prod, prod_r = (S_(n) for n in ("ss", "norm", "tilde", "tilde_T_psum", "tilde_T", "product", "product_out"))
                Mn_r, Y_p, Y_r, X_p, X_r = (S_(n) for n in ("level_mask", "Y_psum", "Y_ready", "X_psum", "X_ready"))
                U_p, U_r, W_p, W_r, sa_p, sa_r, S_p, S_r, y_p = (S_(n) for n in ("U_psum", "U_ready", "W_psum", "W_ready", "sa_psum", "sa_ready", "S_psum", "S_ready", "y_psum"))
                var_r, std_r, y_r, stored, chain_s, msk_r = (S_(n) for n in ("var", "std", "y_ready", "stored", "dve_chain", "masked"))

                with nc.Block() as block:
                    @block.sync
                    def _(sp):
                        rr = i * P + row0
                        sp.dma_start(x[:, :], rows_at(sc["pc"], rr)).then_inc(x_loaded, 16)
                        sp.dma_start(pv[:, :], rows_at(sc["prev"], rr)).then_inc(x_loaded, 16)
                        sp.wait_ge(y_r, 1)
                        sp.dma_start(sc["y"][bass.ds(rr, W), AW + BW:D], yq[0:W, :, :].rearrange("p h d -> p (h d)")).then_inc(stored, 16)
                        sp.wait_ge(stored, 16)

                    @block.scalar
                    def _(act):
                        act.wait_ge(shifted, 1)
                        act.activation(lg[:, 0, 0:HD], x[:, 3 * CW:3 * CW + HD], ACT.Tanh)
                        act.activation(lg[:, 0, HD:P], x[:, 3 * CW + HD:3 * CW + P], ACT.Copy)
                        act.activation(lg[:, 1, :], x[:, 3 * CW + P:C_PROJ], ACT.Sigmoid).then_inc(lora_in, 1)
                        act.wait_ge(lora_p, 1)
                        act.activation(lT[:, :, :], bk[0][:, 0:2 * W].rearrange("p (a t) -> p a t", a=2), ACT.Copy).then_inc(lora_T, 1)
                        act.wait_ge(lora_o, 2)
                        act.activation(gg[0:W, :], bk[2][0:W, 0:CW], ACT.Copy).then_inc(g_out, 1)
                        act.wait_ge(z_r, 1)
                        act.activation(sg[0:W, :, :].rearrange("p a n -> p (a n)"), zz[0:W, :], ACT.Sigmoid).then_inc(sig_r, 1)
                        act.wait_ge(ss_r, 1)
                        act.activation(sm[0:W, 1, :], sm[0:W, 0, :], ACT.Sqrt).then_inc(nrm_r, 1)
                        act.wait_ge(ce_r, 1)
                        act.activation(ex[0:W, 0, :], bk[3][0:W, 0:CW], ACT.Exp)
                        act.activation(ex[0:W, 1, :], bk[3][0:W, 0:CW], ACT.Exp, scale=-1.0)
                        act.activation(ex[0:W, 2, :], ce[0:W, :], ACT.Exp).then_inc(exp_r, 1)
                        act.wait_ge(dc_p, 1)
                        act.activation(dc[:, :, :], bk[4][0:HD, 0:CH * NC].rearrange("p (h c) -> p h c", h=CH), ACT.Exp).then_inc(dc_r, 1)
                        for n, b_ in enumerate((5, 6, 7, 0)):
                            act.wait_ge(tT_p, n + 1)
                            act.activation(tT[:, n, :, :], hw(bk[b_], HD), ACT.Copy).then_inc(tT_r, 1)
                        act.wait_ge(var_r, 1)
                        act.activation(sm[0:W, 5, :], sm[0:W, 4, :], ACT.Sqrt, bias=const["lneps"][0:W, 0:1], scale=1.0 / HD).then_inc(std_r, 1)

                    @block.tensor
                    def _(pe):
                        pe.wait_ge(lora_in, 1)
                        for n in range(2):
                            ins = pe.transpose(bk[0][:, n * W:(n + 1) * W], lg[0:W, n, :], ident[0:W, 0:W])
                        ins.then_inc(lora_p, 1)
                        pe.wait_ge(lora_T, 1)
                        pe.matmul(bk[1][0:W, :], lT[:, 0, :], wa2[:, :], start=True, stop=True).then_inc(lora_o, 1)
                        pe.matmul(bk[2][0:W, 0:CW], lT[:, 1, :], g2[:, :], start=True, stop=True).then_inc(lora_o, 1)
                        pe.wait_ge(ld_r, 1)
                        pe.matmul(bk[3][0:W, 0:CW], masks[0:W, m_incl, 0:W], ld[0:W, :], start=True, stop=True).then_inc(cum_p, 1)
                        which = masks[0:W, CHUNK_OF if G == 1 else SEQ_OF, 0:NC]
                        for hh in range(CH):
                            ins = pe.matmul(bk[4][0:HD, hh * NC:(hh + 1) * NC], ld[0:W, hh * HD:(hh + 1) * HD], which, start=True, stop=True)
                        ins.then_inc(dc_p, 1)
                        for n, b_ in enumerate((5, 6, 7, 0)):
                            pe.wait_ge(til_r, n + 1)
                            for hh in range(CH):
                                ins = pe.transpose(bk[b_][0:HD, hh * W:(hh + 1) * W], til[0:W, n, hh * HD:(hh + 1) * HD], ident[0:W, 0:W])
                            ins.then_inc(tT_p, 1)
                        pe.wait_ge(tT_r, 4)
                        pe.wait_ge(g_out, 1)
                        for b_, a_, c_ in ((1, 1, 0), (2, 0, 1), (3, 2, 0), (5, 1, 3), (6, 2, 3)):
                            for hh in range(CH):
                                ins = pe.matmul(bk[b_][0:W, hh * W:(hh + 1) * W], tT[:, a_, hh, :], tT[:, c_, hh, :], start=True, stop=True)
                            ins.then_inc(prod, 1)
                        for j in range(1, levels):
                            pe.wait_ge(X_r, 2 * j)
                            pe.wait_ge(Mn_r, j)
                            for hh in range(CH):
                                ins = pe.matmul(bk[7][0:W, hh * W:(hh + 1) * W], Mn[0:W, hh, :], X[0:W, hh, :], start=True, stop=True)
                            ins.then_inc(Y_p, 1)
                            pe.wait_ge(Y_r, j)
                            if j == 1:
                                pe.wait_ge(dc_r, 1)
                            if j < levels - 1:
                                for hh in range(CH):
                                    ins = pe.matmul(bk[0][0:W, hh * W:(hh + 1) * W], XT[0:W, hh, :], Y[0:W, hh, :], start=True, stop=True)
                                ins.then_inc(X_p, 1)
                            for hh in range(CH):
                                ins = pe.matmul(bk[4][0:W, hh * W:(hh + 1) * W], Y[0:W, hh, :], XT[0:W, hh, :], start=True, stop=True)
                            ins.then_inc(X_p, 1)
                        pe.wait_ge(prod_r, 5)
                        V = lambda hh: x[0:W, 2 * CW + hh * HD:2 * CW + (hh + 1) * HD]
                        for hh in range(CH):
                            ins = pe.matmul(bk[1][0:W, hh * HD:(hh + 1) * HD], MT[0:W, 0, hh, :], V(hh), start=True, stop=True)
                        ins.then_inc(U_p, 1)
                        pe.wait_ge(X_r, 2 * levels - 1)
                        for hh in range(CH):
                            ins = pe.matmul(bk[3][0:HD, hh * W:(hh + 1) * W], til[0:W, 0, hh * HD:(hh + 1) * HD], XT[0:W, hh, :], start=True, stop=True)
                        ins.then_inc(W_p, 1)
                        pe.wait_ge(U_r, 1)
                        for hh in range(CH):
                            ins = pe.matmul(bk[2][0:W, hh * HD:(hh + 1) * HD], XT[0:W, hh, :], U[0:W, hh, :], start=True, stop=True)
                        ins.then_inc(W_p, 1)
                        pe.wait_ge(W_r, 2)
                        if G == 1:
                            for c in range(NC):
                                cs = slice(c * C, (c + 1) * C)
                                if c:
                                    pe.wait_ge(S_r, c)
                                for hh in range(CH):
                                    ins = pe.matmul(bk[5][cs, hh * HD:(hh + 1) * HD], GT[:, hh, cs], ST[:, hh, 0, :], start=True, stop=True)
                                ins.then_inc(sa_p, 1)
                                for hh in range(CH):
                                    pe.matmul(bk[6][cs, hh * HD:(hh + 1) * HD], tT[:, 3, hh, cs], ST[:, hh, 0, :], start=True, stop=True)
                                pe.wait_ge(sa_r, c + 1)
                                for hh in range(CH):
                                    pe.matmul(bk[7][0:HD, hh * HD:(hh + 1) * HD], til[cs, 1, hh * HD:(hh + 1) * HD], sa[cs, hh, :], start=True, stop=False)
                                    ins = pe.matmul(bk[7][0:HD, hh * HD:(hh + 1) * HD], til[cs, 2, hh * HD:(hh + 1) * HD],
                                                    x[cs, 2 * CW + hh * HD:2 * CW + (hh + 1) * HD], start=False, stop=True)
                                ins.then_inc(S_p, 1)
                        else:
                            pe.wait_ge(msk_r, 1)
                            for hh in range(CH):
                                for bb in range(NG):
                                    ins = pe.matmul(bk[5][0:W, hh * HD:(hh + 1) * HD], gm[:, 0, hh, bb, :], ST[:, hh, bb, :], start=(bb == 0), stop=(bb == NG - 1))
                            ins.then_inc(sa_p, 1)
                            for hh in range(CH):
                                for bb in range(NG):
                                    pe.matmul(bk[6][0:W, hh * HD:(hh + 1) * HD], gm[:, 1, hh, bb, :], ST[:, hh, bb, :], start=(bb == 0), stop=(bb == NG - 1))
                            pe.wait_ge(sa_r, 1)
                            pe.wait_ge(msk_r, 2)
                            for hh in range(CH):
                                for k in range(2):
                                    ins = pe.matmul(bk[(7, 4, 1, 2)[hh]][0:HD, :], til[0:W, 1 + k, hh * HD:(hh + 1) * HD],
                                                    sm_v[0:W, k, hh, :, :].rearrange("p g v -> p (g v)"), start=(k == 0), stop=(k == 1))
                            ins.then_inc(S_p, 1)
                        for hh in range(CH):
                            pe.matmul(bk[0][0:W, hh * HD:(hh + 1) * HD], MT[0:W, 1, hh, :], sa[0:W, hh, :], start=True, stop=False)
                            ins = pe.matmul(bk[0][0:W, hh * HD:(hh + 1) * HD], MT[0:W, 2, hh, :], V(hh), start=False, stop=True)
                        ins.then_inc(y_p, 1)

                    @block.vector
                    def _(dve):
                        chain = Chain(dve, chain_s)
                        R_ = slice(0, W)
                        h4 = lambda t: t.rearrange("p (h d) -> p h d", d=HD)
                        dve.wait_ge(x_loaded, 32)
                        chain(dve.tensor_tensor(dl[:, :], pv[:, :], x[:, :], ALU.subtract))
                        chain(dve.tensor_tensor(dl[:, :], dl[:, :], vec["mu"][:, :], ALU.mult))
                        dve.tensor_tensor(x[:, :], x[:, :], dl[:, :], ALU.add).then_inc(shifted, 1)
                        dve.wait_ge(shifted, 1)
                        chain(dve.tensor_tensor(kk[:, :], x[:, CW:2 * CW], vec["k_k"][:, :], ALU.mult))
                        chain(dve.tensor_tensor(tt[:, :], kk[:, :], kk[:, :], ALU.mult))
                        dve.tensor_reduce(sm[0:W, 0, :], h4(tt[0:W, :]), AX, ALU.add).then_inc(ss_r, 1)
                        dve.wait_ge(lora_o, 1)
                        dve.tensor_tensor(zz[R_, :], bk[1][0:W, :], vec["wa0"][R_, :], ALU.add).then_inc(z_r, 1)
                        dve.wait_ge(nrm_r, 1)
                        chain(dve.tensor_scalar(sm[R_, 2, :], sm[R_, 1, :], 1e-12, None, ALU.max))
                        chain(dve.reciprocal(sm[R_, 3, :], sm[R_, 2, :]))
                        chain(dve.tensor_tensor(h4(kk[R_, :]), h4(kk[R_, :]), sm[R_, 3, :].unsqueeze(2).to_broadcast([W, CH, HD]), ALU.mult))
                        dve.wait_ge(sig_r, 1)
                        dve.tensor_scalar(ld[R_, :], sg[R_, 0, :], -math.exp(-0.5), None, ALU.mult).then_inc(ld_r, 1)
                        chain(dve.scalar_tensor_tensor(out=tt[R_, :], in0=sg[R_, 1, :], scalar=-1.0, in1=vec["k_a"][R_, :], op0=ALU.add, op1=ALU.mult))
                        chain(dve.scalar_tensor_tensor(out=ck[R_, :], in0=tt[R_, :], scalar=1.0, in1=x[R_, CW:2 * CW], op0=ALU.add, op1=ALU.mult))
                        dve.wait_ge(ld_r, 1)
                        dve.wait_ge(cum_p, 1)
                        dve.tensor_tensor(ce[R_, :], bk[3][0:W, 0:CW], ld[R_, :], ALU.subtract).then_inc(ce_r, 1)
                        chain(dve.tensor_tensor(zz[R_, 0:CW], kk[R_, :], sg[R_, 1, :], ALU.mult))
                        chain(dve.tensor_tensor(tt[R_, :], x[R_, 0:CW], ck[R_, :], ALU.mult))
                        chain(dve.tensor_tensor(tt[R_, :], tt[R_, :], vec["r_k"][R_, :], ALU.mult))
                        chain(dve.tensor_reduce(bon[R_, :], h4(tt[R_, :]), AX, ALU.add))
                        dve.wait_ge(exp_r, 1)
                        dve.scalar_tensor_tensor(out=til[R_, 0, :], in0=kk[R_, :], scalar=-1.0, in1=ex[R_, 2, :], op0=ALU.mult, op1=ALU.mult).then_inc(til_r, 1)
                        dve.tensor_tensor(til[R_, 1, :], zz[R_, 0:CW], ex[R_, 1, :], ALU.mult).then_inc(til_r, 1)
                        dve.tensor_tensor(til[R_, 2, :], ck[R_, :], ex[R_, 1, :], ALU.mult).then_inc(til_r, 1)
                        dve.tensor_tensor(til[R_, 3, :], x[R_, 0:CW], ex[R_, 0, :], ALU.mult).then_inc(til_r, 1)
                        dve.wait_ge(prod, 1)
                        chain(dve.tensor_copy(LT[R_, :, :], hw(bk[1])))
                        dve.tensor_tensor(Mn[R_, :, :], LT[R_, :, :], mask4(LEVEL_ST + 1), ALU.mult).then_inc(Mn_r, 1)
                        chain(dve.tensor_tensor(XT[R_, :, :], LT[R_, :, :], mask4(LEVEL_ST), ALU.mult))
                        idb = ident[0:W, 0:W].unsqueeze(1).to_broadcast([W, CH, W])
                        dve.tensor_tensor(XT[R_, :, :], XT[R_, :, :], idb, ALU.add).then_inc(X_r, 1)
                        dve.wait_ge(prod, 2)
                        chain(dve.tensor_tensor(X[R_, :, :], hw(bk[2]), mask4(LEVEL_TS), ALU.mult))
                        dve.tensor_tensor(X[R_, :, :], X[R_, :, :], idb, ALU.add).then_inc(X_r, 1)
                        for j in range(1, levels):
                            if j == 1:
                                for n, (b_, mk) in enumerate(((3, m_strict), (5, m_incl), (6, m_incl))):
                                    dve.wait_ge(prod, 3 + n)
                                    ins = dve.tensor_tensor(MT[R_, n, :, :], hw(bk[b_]), mask4(mk), ALU.mult)
                                    ins.then_inc(prod_r, 1 if n < 2 else 3)
                            dve.wait_ge(Y_p, j)
                            dve.tensor_copy(Y[R_, :, :], hw(bk[7])).then_inc(Y_r, 1)
                            if j < levels - 1:
                                dve.tensor_tensor(Mn[R_, :, :], LT[R_, :, :], mask4(LEVEL_ST + j + 1), ALU.mult).then_inc(Mn_r, 1)
                                dve.wait_ge(X_p, 2 * j)
                                dve.tensor_tensor(X[R_, :, :], hw(bk[0]), X[R_, :, :], ALU.add).then_inc(X_r, 1)
                            else:
                                dve.wait_ge(X_p, 2 * j - 1)
                            dve.tensor_tensor(XT[R_, :, :], hw(bk[4]), XT[R_, :, :], ALU.add).then_inc(X_r, 1)
                        dve.wait_ge(U_p, 1)
                        dve.tensor_copy(U[R_, :, :], hv(bk[1])).then_inc(U_r, 1)
                        dve.wait_ge(W_p, 1)
                        dve.tensor_copy(GT[:, :, :], hw(bk[3], HD)).then_inc(W_r, 1)
                        dve.wait_ge(W_p, 2)
                        dve.tensor_copy(Wv[R_, :, :], hv(bk[2])).then_inc(W_r, 1)
                        dve.wait_ge(W_r, 2)
                        if G == 1:
                            for c in range(NC):
                                cs = slice(c * C, (c + 1) * C)
                                dve.wait_ge(sa_p, c + 1)
                                dve.tensor_tensor(sa[cs, :, :], bk[5][cs, 0:CW].rearrange("p (h v) -> p h v", h=CH), Wv[cs, :, :], ALU.add).then_inc(sa_r, 1)
                                dve.wait_ge(S_p, c + 1)
                                chain(dve.tensor_tensor(ST[:, :, 0, :], hv(bk[7], HD), ST[:, :, 0, :], ALU.add))
                                dve.tensor_tensor(ST[:, :, 0, :], ST[:, :, 0, :], dc[:, :, c:c + 1].to_broadcast([HD, CH, HD]), ALU.mult).then_inc(S_r, 1)
                        else:
                            for k, src in enumerate((GT, tT[:, 3])):
                                for hh in range(CH):
                                    for bb in range(NG):
                                        ins = dve.tensor_copy(gm[:, k, hh, bb, bb * DT:(bb + 1) * DT], src[:, hh, bb * DT:(bb + 1) * DT])
                            ins.then_inc(msk_r, 1)
                            seqm = masks[0:W, SEQ_OF, 0:NG].unsqueeze(2).to_broadcast([W, NG, HD])
                            dve.wait_ge(sa_p, 1)
                            dve.tensor_tensor(sa[R_, :, :], hv(bk[5]), Wv[R_, :, :], ALU.add).then_inc(sa_r, 1)
                            dve.wait_ge(sa_r, 1)
                            for hh in range(CH):
                                dve.tensor_tensor(sm_v[R_, 0, hh, :, :], sa[R_, hh, :].unsqueeze(1).to_broadcast([W, NG, HD]), seqm, ALU.mult)
                                ins = dve.tensor_tensor(sm_v[R_, 1, hh, :, :], x[R_, 2 * CW + hh * HD:2 * CW + (hh + 1) * HD].unsqueeze(1).to_broadcast([W, NG, HD]), seqm, ALU.mult)
                            ins.then_inc(msk_r, 1)
                            dve.wait_ge(S_p, 1)
                            for hh in range(CH):
                                chain(dve.tensor_tensor(ST[:, hh, :, :], bk[(7, 4, 1, 2)[hh]][0:HD, :].rearrange("p (g v) -> p g v", v=HD), ST[:, hh, :, :], ALU.add))
                                dve.tensor_tensor(ST[:, hh, :, :], ST[:, hh, :, :], dc[:, hh, :].unsqueeze(2).to_broadcast([HD, NG, HD]), ALU.mult)
                        dve.wait_ge(y_p, 1)
                        chain(dve.tensor_copy(y[R_, :, :], hv(bk[6])))
                        chain(dve.tensor_tensor(y[R_, :, :], hv(bk[0]), y[R_, :, :], ALU.add))
                        chain(dve.tensor_reduce(sm[R_, 6, :], y[R_, :, :], AX, ALU.add))
                        chain(dve.tensor_scalar(sm[R_, 7, :], sm[R_, 6, :], -1.0 / HD, None, ALU.mult))
                        bc = lambda t: t.unsqueeze(2).to_broadcast([W, CH, HD])
                        chain(dve.tensor_tensor(y[R_, :, :], y[R_, :, :], bc(sm[R_, 7, :]), ALU.add))
                        chain(dve.tensor_tensor(yq[R_, :, :], y[R_, :, :], y[R_, :, :], ALU.mult))
                        dve.tensor_reduce(sm[R_, 4, :], yq[R_, :, :], AX, ALU.add).then_inc(var_r, 1)
                        dve.wait_ge(std_r, 1)
                        chain(dve.reciprocal(sm[R_, 8, :], sm[R_, 5, :]))
                        chain(dve.tensor_tensor(y[R_, :, :], y[R_, :, :], bc(sm[R_, 8, :]), ALU.mult))
                        chain(dve.tensor_tensor(y[R_, :, :], y[R_, :, :], h4(vec["ln_w"][R_, :]), ALU.mult))
                        chain(dve.tensor_tensor(y[R_, :, :], y[R_, :, :], h4(vec["ln_b"][R_, :]), ALU.add))
                        chain(dve.tensor_tensor(yq[R_, :, :], h4(x[R_, 2 * CW:3 * CW]), bc(bon[R_, :]), ALU.mult))
                        chain(dve.tensor_tensor(y[R_, :, :], y[R_, :, :], yq[R_, :, :], ALU.add))
                        dve.wait_ge(g_out, 1)
                        dve.tensor_tensor(yq[R_, :, :], y[R_, :, :], h4(gg[R_, :]), ALU.mult).then_inc(y_r, 1)
                st.close_sems()

            if tiles > 1:
                with nc.Fori(0, tiles) as i:
                    body(i)
            else:
                body(0)

            turned = st.sem("turned")
            copied = st.sem("copied")
            stored = st.sem("stored")
            with nc.Block() as block:
                @block.tensor
                def _(pe):
                    for bb in range(NG):
                        if bb >= 2:
                            pe.wait_ge(copied, bb - 1)
                        for k in range(CH):
                            ins = pe.transpose(bk[bb % 2][0:HD, k * HD:(k + 1) * HD], ST[:, k, bb, :], ident[0:HD, 0:HD])
                        ins.then_inc(turned, 1)

                @block.vector
                def _(dve):
                    for bb in range(NG):
                        dve.wait_ge(turned, bb + 1)
                        dve.tensor_copy(nat[:, bb, :, :], hv(bk[bb % 2], HD)).then_inc(copied, 1)

                @block.sync
                def _(sp):
                    sp.wait_ge(copied, NG)
                    for bb in range(NG):
                        sp.dma_start(layer(io[tag + "_rwkv_S"], l)[bb].rearrange("h v k -> v h k"), nat[:, bb]).then_inc(stored, 16)
                    sp.wait_ge(stored, 16 * NG)

    group(1, P, NT, 0, "p")
    group(DB, NS, 1, SEQ, "s")


def stage_prompt_dsa(nc, l, io, sc, const):
    STRUCK = -3e38
    with Stage(nc) as st:
        kT = st.sb("kT", [P, 2, SEQ])
        ikT = st.sb("ikT", [P, SEQ])
        v = st.sb("v", [P, NT, KVH * HD])
        qT = st.sb("qT", [P, 4, P])
        iqT = st.sb("iqT", [P, 4, P])
        iw = st.sb("iw", [P, 2, IH])
        rl = [st.sb(f"relu{b}", [P, SEQ]) for b in range(2)]
        acc = st.sb("score", [P, SEQ])
        bias = st.sb("sel_bias", [P, SEQ])
        top = st.sb("top8", [P, 8])
        s = [st.sb(f"s{b}", [P, SEQ]) for b in range(2)]
        pr = [st.sb(f"p{b}", [P, SEQ]) for b in range(2)]
        pT = [st.sb(f"pT{b}", [P, NT, P]) for b in range(2)]
        mx = st.sb("mx", [P, 4, BH])
        o = st.sb("o", [P, BH, HD])
        ps = [st.ps(f"ps{b}", [P, 2, 512]) for b in range(2)]
        pt = st.ps("pt", [P, 2, 4, P])
        po = [st.ps(f"po{b}", [P, 512]) for b in range(2)]
        ident = const["ident"]

        loaded = st.sem("loaded")
        with nc.Block() as block:
            @block.sync
            def _(sp):
                sp.dma_start(kT[:, :, :], sc["kT"][:, :, 0:SEQ].rearrange("a p n -> p a n")).then_inc(loaded, 16)
                sp.dma_start(ikT[:, :], sc["ikT"][:, 0:SEQ]).then_inc(loaded, 16)
                sp.dma_start(v[:, :, :], sc["v"][0:SEQ, :].rearrange("(t p) n -> p t n", p=P)).then_inc(loaded, 16)
                sp.wait_ge(loaded, 48)
        st.close_sems()

        def tile(i):
            N = (i + 1) * P
            chunks = [(c, min(512, N - c)) for c in range(0, N, 512)]
            nch = len(chunks)
            q_loaded, idx_p, idx_r, idx_used, sel_r = (st.sem(n) for n in ("q_loaded", "idx_psum", "idx_relu", "idx_added", "selected"))
            s_p, s_r, mx_r, p_r, pt_p, pt_a, pt_d, o_p, o_r, stored, chain_s = (st.sem(n) for n in (
                "s_psum", "s_ready", "max_ready", "p_ready", "pT_psum", "pT_act", "pT_dve", "o_psum", "o_ready", "stored", "dve_chain"))
            with nc.Block() as block:
                @block.sync
                def _(sp):
                    c = slice(i * P, (i + 1) * P)
                    sp.dma_start(iqT[:, :, :], sc["iqT"][:, :, c].rearrange("a p n -> p a n")).then_inc(q_loaded, 16)
                    sp.dma_start(iw[:, 0, :], sc["iw"][c, :]).then_inc(q_loaded, 16)
                    sp.dma_start(qT[:, :, :], sc["qT"][:, :, c].rearrange("a p n -> p a n")).then_inc(q_loaded, 16)
                    sp.wait_ge(o_r, BH)
                    sp.dma_start(sc["y"][c, AW:AW + BW], o[:, :, :].rearrange("p h d -> p (h d)")).then_inc(stored, 16)
                    sp.wait_ge(stored, 16)

                @block.tensor
                def _(pe):
                    pe.wait_ge(q_loaded, 48)
                    for h in range(IH):
                        e = slice(HD * (h % 2), HD * (h % 2) + HD)
                        if h >= 2:
                            pe.wait_ge(idx_r, h - 1)
                        for n, (c0, cw) in enumerate(chunks):
                            ins = pe.matmul(ps[h % 2][:, n, 0:cw], iqT[e, h // 2, :], ikT[e, c0:c0 + cw], start=True, stop=True)
                        ins.then_inc(idx_p, 1)

                    def score(h):
                        kv, g = h // 2, h % 2
                        e = slice(HD * (kv % 2), HD * (kv % 2) + HD)
                        if h < 2:
                            pe.wait_ge(idx_r, IH - 1 + h)
                        else:
                            pe.wait_ge(s_r, h - 1)
                        for n, (c0, cw) in enumerate(chunks):
                            ins = pe.matmul(ps[h % 2][:, n, 0:cw], qT[e, kv // 2 * 2 + g, :], kT[e, kv // 2, c0:c0 + cw], start=True, stop=True)
                        ins.then_inc(s_p, 1)

                    score(0)
                    for h in range(BH):
                        if h + 1 < BH:
                            score(h + 1)
                        pe.wait_ge(p_r, h + 1)
                        if h:
                            pe.wait_ge(pt_a, h)
                            if nch > 1:
                                pe.wait_ge(pt_d, h)
                        for k in range(i + 1):
                            ins = pe.transpose(pt[:, k // 4, k % 4, :], pr[h % 2][:, k * P:(k + 1) * P], ident[:, :])
                        ins.then_inc(pt_p, 1)
                        pe.wait_ge(pt_a, h + 1)
                        if nch > 1:
                            pe.wait_ge(pt_d, h + 1)
                        if h >= 2:
                            pe.wait_ge(o_r, h - 1)
                        for k in range(i + 1):
                            ins = pe.matmul(po[h % 2][:, 0:HD], pT[h % 2][:, k, :], v[:, k, h // 2 * HD:(h // 2 + 1) * HD], start=(k == 0), stop=(k == i))
                        ins.then_inc(o_p, 1)

                @block.scalar
                def _(act):
                    for h in range(IH):
                        act.wait_ge(idx_p, h + 1)
                        if h >= 2:
                            act.wait_ge(idx_used, h - 1)
                        act.activation(rl[h % 2][:, 0:N], ps[h % 2][:, :, :].rearrange("p a n -> p (a n)")[:, 0:N], ACT.Relu, scale=HD ** -0.5).then_inc(idx_r, 1)
                    for h in range(BH):
                        act.wait_ge(mx_r, h + 1)
                        if h >= 2:
                            act.wait_ge(pt_p, h - 1)
                        act.activation(pr[h % 2][:, 0:N], s[h % 2][:, 0:N], ACT.Exp, bias=mx[:, 1, h:h + 1], scale=HD ** -0.5,
                                       accum_out=mx[:, 2, h:h + 1]).then_inc(p_r, 1)
                        act.wait_ge(pt_p, h + 1)
                        if h >= 2:
                            act.wait_ge(o_p, h - 1)
                        m = min(4, i + 1)
                        act.activation(pT[h % 2][:, 0:m, :], pt[:, 0, 0:m, :], ACT.Copy).then_inc(pt_a, 1)

                @block.vector
                def _(dve):
                    chain = Chain(dve, chain_s)
                    dve.wait_ge(q_loaded, 48)
                    chain(dve.tensor_scalar(iw[:, 1, :], iw[:, 0, :], IH ** -0.5, None, ALU.mult))
                    for h in range(IH):
                        dve.wait_ge(idx_r, h + 1)
                        if h == 0:
                            ins = dve.tensor_scalar(acc[:, 0:N], rl[0][:, 0:N], iw[:, 1, 0:1], None, ALU.mult)
                        else:
                            dve.wait_ge(idx_used, h)
                            ins = dve.scalar_tensor_tensor(out=acc[:, 0:N], in0=rl[h % 2][:, 0:N], scalar=iw[:, 1, h:h + 1], in1=acc[:, 0:N],
                                                           op0=ALU.mult, op1=ALU.add)
                        ins.then_inc(idx_used, 1)
                    dve.wait_ge(idx_used, IH)
                    if N > TOPK:
                        chain(dve.tensor_tensor(acc[:, N - P:N], acc[:, N - P:N], const["masks"][:, CAUSAL_QK, :], ALU.add))
                        for k in range(TOPK // 8):
                            chain(dve.max(top[:, :], acc[:, 0:N]))
                            chain(dve.match_replace(acc[:, 0:N], top[:, :], acc[:, 0:N], STRUCK))
                        chain(dve.tensor_scalar(bias[:, 0:N], acc[:, 0:N], STRUCK / 2, NEG, ALU.is_gt, ALU.mult))
                    else:
                        chain(dve.memset(bias[:, 0:N], 0.0))
                        chain(dve.tensor_copy(bias[:, N - P:N], const["masks"][:, CAUSAL_QK, :]))

                    def mask_and_max(h):
                        dve.wait_ge(s_p, h + 1)
                        if h >= 2:
                            dve.wait_ge(p_r, h - 1)
                        dve.tensor_tensor_reduce(s[h % 2][:, 0:N], ps[h % 2][:, :, :].rearrange("p a n -> p (a n)")[:, 0:N], bias[:, 0:N],
                                                 1.0, STRUCK, ALU.add, ALU.max, mx[:, 0, h:h + 1]).then_inc(s_r, 1)
                        dve.wait_ge(s_r, h + 1)
                        dve.tensor_scalar(mx[:, 1, h:h + 1], mx[:, 0, h:h + 1], -HD ** -0.5, None, ALU.mult).then_inc(mx_r, 1)

                    mask_and_max(0)
                    for h in range(BH):
                        if h + 1 < BH:
                            mask_and_max(h + 1)
                        if nch > 1:
                            dve.wait_ge(pt_p, h + 1)
                            if h >= 2:
                                dve.wait_ge(o_p, h - 1)
                            dve.tensor_copy(pT[h % 2][:, 4:i + 1, :], pt[:, 1, 0:i - 3, :]).then_inc(pt_d, 1)
                        dve.wait_ge(p_r, h + 1)
                        chain(dve.reciprocal(mx[:, 3, h:h + 1], mx[:, 2, h:h + 1]))
                        dve.wait_ge(o_p, h + 1)
                        dve.tensor_scalar(o[:, h, :], po[h % 2][:, 0:HD], mx[:, 3, h:h + 1], None, ALU.mult).then_inc(o_r, 1)
            st.close_sems()

        for i in range(NT):
            tile(i)


OFFS = 16
RUNS = PAGE // OFFS
SUB = 4
GT_ = HALF // P
STRUCK_OUT = -3e38


def stage_sample_index(nc, l, io, sc, const):
    table = io["cache_idx_k"].rearrange("l n (c o) d -> (l n c) (o d)", o=OFFS)
    with Stage(nc) as st:
        ik = [st.sb(f"ik{n}", [P, OFFS * HD]) for n in range(4)]
        idx = st.sb("idx", [P, 4], U32)
        iq = st.sb("iq_diag", [P, 2, IH, DT])
        ikn = st.sb("ik_new", [HD, NS])
        iwc = st.sb("iw_col", [P, 2])
        pk = st.sb("pick", [P, 2, DT])
        kt = [st.sb(f"ikT{b}", [P, 4, P]) for b in range(2)]
        rl = [st.sb(f"relu{b}", [P, 512]) for b in range(2)]
        rown = st.sb("row_new", [DT, NS])
        rows = st.sb("row", [DT, 2, HALF])
        pt = [st.ps(f"pt{b}", [P, 4, P]) for b in range(2)]
        pi = [st.ps(f"pi{b}", [P, 512]) for b in range(2)]
        pw = [st.ps(f"pw{b}", [DT, 2, 512]) for b in range(2)]
        ident = const["ident"]
        zeroed = st.sem("zeroed")
        chain_s = st.sem("dve_chain")
        loaded = st.sem("loaded")
        pages = st.sb("pages", [P, 2 * DB], I32)
        with nc.Block() as block:
            @block.sync
            def _(sp):
                sp.dma_start(pages[:, :], io["pages"]).then_inc(loaded, 16)
                sp.dma_start(ikn[:, :], sc["ikT"][0:HD, SEQ:SEQ + NS]).then_inc(loaded, 16)
                sp.wait_ge(loaded, 32)

            @block.vector
            def _(dve):
                chain = Chain(dve, chain_s)
                dve.memset(iq[:, :, :, :], 0.0)
                dve.wait_ge(loaded, 32)
                pf = st.sb("pages_f", [P, 2 * DB])
                chain(dve.tensor_copy(pf[:, :], pages[:, :]))
                chain(dve.tensor_scalar(pf[:, :], pf[:, :], float(RUNS), const["lbase"][:, 0:1], ALU.mult, ALU.add))
                for j in range(2):
                    dve.tensor_scalar(const["runs"][:, :, j], pf[:, :], const["sub"][:, j:j + 1], None, ALU.add)
                chain(dve.tensor_scalar(const["lbase"][:, :], const["lbase"][:, :], float(io["cache_k"].shape[1] * RUNS), None, ALU.add))
        st.close_sems()

        with nc.Fori(0, DB) as b:
            (idx_r, got0, got1, got2, got3, q_loaded, pk_r, kt_p, kt_r, i_p, i_r, w_p, w_r, n_p, n_r, nw_p, nw_r, stored, chain_s) = (st.sem(n) for n in (
                "idx_ready", "got0", "got1", "got2", "got3", "q_loaded", "pick_ready", "kT_psum", "kT_ready", "idx_psum", "relu_ready", "sum_psum", "sum_ready",
                "new_psum", "new_relu", "new_sum", "new_ready", "stored", "dve_chain"))
            got = [got0, got1, got2, got3]
            with nc.Block() as block:
                @block.gpsimd
                def _(pool):
                    pool.wait_ge(idx_r, 1)
                    for n in range(4):
                        pool.indirect_dma_start(ik[n][:, :], None, table, bass.IndirectOffsetOnAxis(ap=idx[:, n:n + 1], axis=0)).then_inc(got[n], 16)

                @block.sync
                def _(sp):
                    c = bass.ds(b * DT + SEQ, DT)
                    with nc.allow_non_contiguous_dma(reason="a few words"):
                        for o2 in range(2):
                            for e in range(2):
                                for j in range(4):
                                    sp.dma_start(iq[HD * o2:HD * o2 + HD, o2, 2 * j + e, :], sc["iqT"][j, HD * e:HD * e + HD, c]).then_inc(q_loaded, 16)
                            for h in range(IH):
                                r = HD * o2 + DT * h
                                sp.dma_start(iwc[r:r + DT, 0:1], sc["iw"][c, h:h + 1]).then_inc(q_loaded, 16)
                    sp.wait_ge(w_r, 16)
                    sp.wait_ge(nw_r, 1)
                    for f in range(2):
                        sp.dma_start(sc["score"][bass.ds(b * DT + f * NS, DT), :], rows[:, f, :]).then_inc(stored, 16)
                    sp.dma_start(sc["score_new"][bass.ds(b * DT, DT), :], rown[:, :]).then_inc(stored, 16)
                    sp.wait_ge(stored, 48)

                @block.tensor
                def _(pe):
                    pe.wait_ge(q_loaded, 16 * 32)
                    pe.matmul(pi[0][0:HD, 0:NS], iq[0:HD, 0, :, :].rearrange("p h t -> p (h t)"), ikn[:, :], start=True, stop=True).then_inc(n_p, 1)
                    pe.wait_ge(pk_r, 1)
                    pe.wait_ge(n_r, 1)
                    pe.matmul(pw[0][:, 0, 0:NS], pk[0:HD, 0, :], rl[1][0:HD, 0:NS], start=True, stop=True).then_inc(nw_p, 1)
                    pe.wait_ge(nw_r, 1)

                    def turn(m):
                        if m % 2 == 0:
                            pe.wait_ge(got[m // 2], 16)
                        if m >= 2:
                            pe.wait_ge(kt_r, m - 1)
                        for k in range(4):
                            o = (m % 2) * 8 + 2 * k
                            ins = pe.transpose(pt[m % 2][:, k, :], ik[m // 2][:, o * HD:(o + 2) * HD], ident[:, :])
                        ins.then_inc(kt_p, 1)

                    def score(m):
                        pe.wait_ge(kt_r, m + 1)
                        if m >= 2:
                            pe.wait_ge(i_r, m - 1)
                        pe.matmul(pi[m % 2][:, :], iq[:, :, :, :].rearrange("p a h t -> p (a h t)"), kt[m % 2][:, :, :], start=True, stop=True).then_inc(i_p, 1)

                    def weigh(m):
                        pe.wait_ge(i_r, m + 1)
                        if m >= 2:
                            pe.wait_ge(w_r, 2 * (m - 1))
                        for o2 in range(2):
                            ins = pe.matmul(pw[m % 2][:, o2, :], pk[:, o2, :], rl[m % 2][:, :], start=True, stop=True)
                        ins.then_inc(w_p, 1)

                    turn(0)
                    turn(1)
                    for m in range(8):
                        score(m)
                        if m + 2 < 8:
                            turn(m + 2)
                        if m:
                            weigh(m - 1)
                    weigh(7)

                @block.scalar
                def _(act):
                    act.wait_ge(n_p, 1)
                    act.activation(rl[1][0:HD, 0:NS], pi[0][0:HD, 0:NS], ACT.Relu, scale=HD ** -0.5).then_inc(n_r, 1)
                    for m in range(8):
                        act.wait_ge(i_p, m + 1)
                        if m >= 2:
                            act.wait_ge(w_p, m - 1)
                        elif m == 1:
                            act.wait_ge(nw_p, 1)
                        act.activation(rl[m % 2][:, :], pi[m % 2][:, :], ACT.Relu, scale=HD ** -0.5).then_inc(i_r, 1)

                @block.vector
                def _(dve):
                    chain = Chain(dve, chain_s)
                    dve.tensor_copy(idx[:, :], const["runs"][:, bass.ds(b * 2, 2), :].rearrange("p f j -> p (f j)")).then_inc(idx_r, 1)
                    dve.wait_ge(q_loaded, 16 * 32)
                    chain(dve.tensor_scalar(iwc[:, 1:2], iwc[:, 0:1], IH ** -0.5, None, ALU.mult))
                    dve.tensor_scalar(pk[:, :, :].rearrange("p a t -> p (a t)"), const["masks"][:, PICK, 0:2 * DT], iwc[:, 1:2], None, ALU.mult).then_inc(pk_r, 1)
                    dve.wait_ge(nw_p, 1)
                    dve.tensor_copy(rown[:, :], pw[0][:, 0, 0:NS]).then_inc(nw_r, 1)

                    def copy_kt(m):
                        dve.wait_ge(kt_p, m + 1)
                        if m >= 2:
                            dve.wait_ge(i_p, m - 1)
                        dve.tensor_copy(kt[m % 2][:, :, :], pt[m % 2][:, :, :]).then_inc(kt_r, 1)

                    def place(m):
                        f, j, hi = m // 4, m // 2 % 2, m % 2
                        dve.wait_ge(w_p, m + 1)
                        for o2 in range(2):
                            dst = rows[:, f, :].rearrange("p (g j c o k q) -> p j o k q g c", g=32, j=2, c=SUB, o=2, k=4)[:, j, hi, :, o2, :, :]
                            dve.tensor_copy(dst, pw[m % 2][:, o2, :].rearrange("p (k g c) -> p k g c", k=4, g=32)).then_inc(w_r, 1)

                    copy_kt(0)
                    copy_kt(1)
                    for m in range(8):
                        if m >= 1:
                            place(m - 1)
                        if m + 2 < 8:
                            copy_kt(m + 2)
                    place(7)
            st.close_sems()


def stage_sample_select(nc, l, io, sc, const):
    with Stage(nc) as st:
        s = st.sb("s", [P, HALF])
        wk = st.sb("work", [P, HALF])
        eq = st.sb("eq", [P, HALF])
        ones = st.sb("ones_row", [P, HALF])
        cand = st.sb("cand", [P, TOPK])
        cm = st.sb("cand_all", [NS, 2 * TOPK + NS])
        cw = st.sb("cand_work", [NS, 2 * TOPK + NS])
        tmp = st.sb("tmp", [NS, TOPK])
        top = st.sb("top8", [NS, 8])
        cnt = st.sb("counts", [NS, 8])
        thr = st.sb("thr", [P, 2])
        bn = st.sb("bias_new", [NS, NS])
        loaded, cand_r, moved, merged, spread, sel_r, stored, chain_s, new_r = (st.sem(n) for n in (
            "loaded", "cand_ready", "moved", "merged", "spread", "sel_ready", "stored", "dve_chain", "new_ready"))
        with nc.Block() as block:
            @block.sync
            def _(sp):
                for q in range(4):
                    sp.dma_start(s[:, q * 1024:(q + 1) * 1024], sc["score"][:, q * 1024:(q + 1) * 1024]).then_inc(loaded, 16)
                sp.dma_start(cm[:, 2 * TOPK:], sc["score_new"]).then_inc(loaded, 16)
                sp.wait_ge(cand_r, 1)
                sp.dma_start(cm[:, 0:TOPK], cand[0:NS, :]).then_inc(moved, 16)
                sp.dma_start(cm[:, TOPK:2 * TOPK], cand[NS:P, :]).then_inc(moved, 16)
                sp.wait_ge(merged, 1)
                sp.dma_start(thr[0:NS, :], cnt[:, 0:2]).then_inc(spread, 16)
                sp.dma_start(thr[NS:P, :], cnt[:, 2:4]).then_inc(spread, 16)
                sp.wait_ge(new_r, 1)
                sp.dma_start(sc["bias_new"], bn[:, :]).then_inc(stored, 16)
                sp.wait_ge(sel_r, 2)
                for j in range(2):
                    sp.dma_start(sc["bias"][:, j * HALF // 2:(j + 1) * HALF // 2], wk[:, j * HALF // 2:(j + 1) * HALF // 2]).then_inc(stored, 16)
                sp.wait_ge(stored, 48)

            @block.vector
            def _(dve):
                chain = Chain(dve, chain_s)
                dve.memset(ones[:, :], 1.0)
                dve.wait_ge(loaded, 80)
                chain(dve.tensor_copy(wk[:, :], s[:, :]))
                for k in range(TOPK // 8):
                    chain(dve.max(cand[:, 8 * k:8 * k + 8], wk[:, :]))
                    ins = dve.match_replace(wk[:, :], cand[:, 8 * k:8 * k + 8], wk[:, :], STRUCK_OUT)
                    if k < TOPK // 8 - 1:
                        chain(ins)
                ins.then_inc(cand_r, 1)
                dve.wait_ge(moved, 32)
                chain(dve.tensor_tensor(cm[:, 2 * TOPK:], cm[:, 2 * TOPK:], const["masks"][0:NS, CAUSAL_QK8, 0:NS], ALU.add))
                chain(dve.tensor_copy(cw[:, :], cm[:, :]))
                for k in range(TOPK // 8):
                    chain(dve.max(top[:, :], cw[:, :]))
                    chain(dve.match_replace(cw[:, :], top[:, :], cw[:, :], STRUCK_OUT))
                dve.tensor_scalar(bn[:, :], cw[:, 2 * TOPK:], STRUCK_OUT / 2, NEG, ALU.is_gt, ALU.mult).then_inc(new_r, 1)
                for f in range(2):
                    c = slice(f * TOPK, (f + 1) * TOPK)
                    dve.tensor_copy(cnt[:, 2 * f:2 * f + 1], top[:, 7:8])
                    chain(dve.tensor_scalar(tmp[:, :], cw[:, c], STRUCK_OUT / 2, 0.0, ALU.is_lt, ALU.add, accum_out=cnt[:, 4:5]))
                    chain(dve.tensor_scalar(tmp[:, :], cm[:, c], top[:, 7:8], 0.0, ALU.is_gt, ALU.add, accum_out=cnt[:, 5:6]))
                    chain(dve.tensor_tensor(cnt[:, 2 * f + 1:2 * f + 2], cnt[:, 4:5], cnt[:, 5:6], ALU.subtract))
                dve.tensor_copy(tmp[:, 0:1], cnt[:, 0:1]).then_inc(merged, 1)
                dve.wait_ge(spread, 32)
                chain(dve.tensor_scalar(eq[:, :], s[:, :], thr[:, 0:1], None, ALU.is_equal))
                chain(dve.tensor_tensor_scan(wk[:, :], ones[:, :], eq[:, :], 0.0, ALU.mult, ALU.add))
                chain(dve.scalar_tensor_tensor(out=eq[:, :], in0=wk[:, :], scalar=thr[:, 1:2], in1=eq[:, :], op0=ALU.is_le, op1=ALU.mult))
                chain(dve.scalar_tensor_tensor(out=eq[:, :], in0=s[:, :], scalar=thr[:, 0:1], in1=eq[:, :], op0=ALU.is_gt, op1=ALU.add))
                for j in range(2):
                    src = eq[:, :].rearrange("p (g j c o) -> p j o g c", g=32, j=2, c=SUB)[:, j]
                    dst = wk[:, j * HALF // 2:(j + 1) * HALF // 2].rearrange("p (o g c) -> p o g c", o=OFFS, g=32)
                    dve.tensor_scalar(dst, src, -1.0, -NEG, ALU.add, ALU.mult).then_inc(sel_r, 1)


def stage_sample_attend(nc, l, io, sc, const):
    tk = io["cache_k"].rearrange("l n (c o) h d -> (l n c) (o h d)", o=OFFS)
    tv = io["cache_v"].rearrange("l n (c o) h d -> (l n c) (o h d)", o=OFFS)
    KW = KVH * HD
    NR = BH * DT
    NTL = 2 * GT_ + 1
    RING = 6
    with Stage(nc) as st:
        ring = [st.sb(f"kv{n}", [P, OFFS * KW]) for n in range(RING)]
        idx = st.sb("idx", [P, 4], U32)
        bl = st.sb("bias_rows", [DT, 2, HALF])
        bnl = st.sb("bias_new", [DT, NS])
        bT = st.sb("biasT", [P, NTL, DT])
        q = st.sb("q_diag", [P, 2, 2, 2, DT])
        kn = st.sb("k_new", [P, 2, NS])
        vn = st.sb("v_new", [NS, KW])
        kt = [st.sb(f"kT{b}", [P, 4, P]) for b in range(2)]
        S = st.sb("S", [P, NTL, NR])
        mx = st.sb("mx", [P, NR])
        mr = st.sb("mx_row", [NR, 4])
        dg = st.sb("diag", [NR, NR])
        dsum = st.sb("dsum", [P, NR])
        om = st.sb("o_masked", [NR, KVH, HD])
        o = st.sb("o", [NR, 2, HD])
        pt = [st.ps(f"pt{b}", [P, 4, P]) for b in range(2)]
        pS = [st.ps(f"pS{b}", [P, 8, NR]) for b in range(2)]
        pb = st.ps("pb", [P, 2 * GT_, DT])
        pm = st.ps("pm", [P, 512])
        po = st.ps("po", [NR, KVH, HD])
        ident = const["ident"]
        loaded = st.sem("loaded")
        zeroed = st.sem("zeroed")
        with nc.Block() as block:
            @block.sync
            def _(sp):
                sp.dma_start(kn[:, :, :], sc["kT"][:, :, SEQ:SEQ + NS].rearrange("a p n -> p a n")).then_inc(loaded, 16)
                sp.dma_start(vn[:, :], sc["v"][SEQ:SEQ + NS, :]).then_inc(loaded, 16)
                sp.wait_ge(loaded, 32)

            @block.vector
            def _(dve):
                dve.memset(q[:, :, :, :, :], 0.0).then_inc(zeroed, 1)
        st.close_sems()

        with nc.Fori(0, DB) as b:
            (idx_r, q_loaded, b_loaded, kt_p, kt_d, kt_c, s_p, s_r, b_p, b_r, n_p, mx_r, mxT_p, mr_r, nm_p, sub_r, e_r, den_r, den_p, o_p, o_m, y_r, stored, chain_s, b_pn, dg_r) = (st.sem(n) for n in (
                "idx_ready", "q_loaded", "bias_loaded", "kT_psum", "kT_even", "kT_odd", "s_psum", "s_ready", "bias_psum", "bias_ready", "new_psum", "mx_ready", "mxT_psum",
                "mx_row_ready", "nm_psum", "sub_ready", "exp_ready", "den_ready", "den_psum", "o_psum", "o_masked", "y_ready", "stored", "dve_chain", "bias_new_psum", "diag_ready"))
            def place_scores(dve, bank):
                dve.wait_ge(s_p, 4 * (bank + 1))
                dve.tensor_tensor(S[:, 8 * bank:8 * bank + 8, :].rearrange("p n (r t) -> p n r t", t=DT),
                                  pS[bank % 2][:, :, :].rearrange("p n (r t) -> p n r t", t=DT),
                                  bT[:, 8 * bank:8 * bank + 8, :].unsqueeze(2).to_broadcast([P, 8, BH, DT]), ALU.add).then_inc(s_r, 1)

            got = [st.sem(f"got{n}") for n in range(8)]
            with nc.Block() as block:
                @block.gpsimd
                def _(pool):
                    pool.wait_ge(idx_r, 1)
                    for n in range(8):
                        if n >= RING:
                            pool.wait_ge(kt_p, 8 * (n - RING + 1))
                        t = tk if n < 4 else tv
                        pool.indirect_dma_start(ring[n % RING][:, :], None, t, bass.IndirectOffsetOnAxis(ap=idx[:, n % 4:n % 4 + 1], axis=0)).then_inc(got[n], 16)

                @block.sync
                def _(sp):
                    c = bass.ds(b * DT + SEQ, DT)
                    for f in range(2):
                        sp.dma_start(bl[:, f, :], sc["bias"][bass.ds(b * DT + f * NS, DT), :]).then_inc(b_loaded, 16)
                    sp.dma_start(bnl[:, :], sc["bias_new"][bass.ds(b * DT, DT), :]).then_inc(b_loaded, 16)
                    with nc.allow_non_contiguous_dma(reason="a few words"):
                        for e in range(2):
                            for a in range(2):
                                for g in range(2):
                                    sp.dma_start(q[HD * e:HD * e + HD, a, e, g, :], sc["qT"][a * 2 + g, HD * e:HD * e + HD, c]).then_inc(q_loaded, 16)
                    sp.wait_ge(y_r, 1)
                    for h in range(BH):
                        sp.dma_start(sc["y"][c, AW + h * HD:AW + (h + 1) * HD], o[h * DT:(h + 1) * DT, 1, :]).then_inc(stored, 16)
                    sp.wait_ge(stored, 16 * BH)

                @block.tensor
                def _(pe):
                    pe.wait_ge(b_loaded, 48)
                    for n in range(2 * GT_):
                        ins = pe.transpose(pb[:, n, :], bl[:, n // GT_, n % GT_ * P:(n % GT_ + 1) * P], ident[0:DT, 0:DT])
                    ins.then_inc(b_p, 1)
                    pe.transpose(pm[0:NS, 0:DT], bnl[:, :], ident[0:DT, 0:DT]).then_inc(b_pn, 1)
                    pe.wait_ge(q_loaded, 128)
                    pe.wait_ge(b_r, 2)
                    qd = lambda a: q[:, a, :, :, :].rearrange("p e g t -> p (e g t)")
                    for a in range(2):
                        ins = pe.matmul(pm[0:NS, 64 + 32 * a:96 + 32 * a], kn[:, a, :], qd(a), start=True, stop=True)
                    ins.then_inc(n_p, 1)

                    def turn(m):
                        n = m // 8
                        if m % 8 == 0:
                            pe.wait_ge(got[n], 16)
                        if m >= 2:
                            pe.wait_ge(kt_c if m % 2 else kt_d, m // 2)
                        for k in range(4):
                            r = (m % 8 * 2) * KW + k * P
                            ins = pe.transpose(pt[m % 2][:, k, :], ring[n][:, r:r + P], ident[:, :])
                        ins.then_inc(kt_p, 1)

                    turn(0)
                    for m in range(32):
                        if m + 1 < 32:
                            turn(m + 1)
                        pe.wait_ge(kt_c if m % 2 else kt_d, m // 2 + 1)
                        bank = m // 4
                        if m % 4 == 0 and bank >= 2:
                            pe.wait_ge(s_r, bank - 1)
                        for k in range(4):
                            ins = pe.matmul(pS[bank % 2][:, m % 4 * 2 + k // 2, 32 * (k % 2):32 * (k % 2) + 32], kt[m % 2][:, k, :], qd(k % 2), start=True, stop=True)
                        ins.then_inc(s_p, 1)
                    pe.wait_ge(mx_r, 1)
                    pe.transpose(pm[0:NR, 128:256], mx[:, :], ident[:, :]).then_inc(mxT_p, 1)
                    pe.wait_ge(dg_r, 1)
                    pe.matmul(pm[:, 256:256 + NR], const["ones"][0:NR, :], dg[:, :], start=True, stop=True).then_inc(nm_p, 1)
                    pe.wait_ge(e_r, 1)
                    for n in range(2 * GT_):
                        if n % OFFS == 0:
                            pe.wait_ge(got[4 + n // OFFS], 16)
                        pe.matmul(po[:, :, :].rearrange("p k d -> p (k d)"), S[:, n, :], ring[(4 + n // OFFS) % RING][:, n % OFFS * KW:(n % OFFS + 1) * KW],
                                  start=(n == 0), stop=False)
                    pe.matmul(po[:, :, :].rearrange("p k d -> p (k d)"), S[0:NS, NTL - 1, :], vn[:, :], start=False, stop=True).then_inc(o_p, 1)
                    pe.wait_ge(den_r, 1)
                    pe.matmul(pm[0:NR, 400:401], dsum[:, :], const["ones"][:, 0:1], start=True, stop=True).then_inc(den_p, 1)

                @block.scalar
                def _(act):
                    for m in range(1, 32, 2):
                        act.wait_ge(kt_p, m + 1)
                        if m >= 3:
                            act.wait_ge(s_p, m - 1)
                        act.activation(kt[1][:, :, :], pt[1][:, :, :], ACT.Copy).then_inc(kt_c, 1)
                    act.wait_ge(sub_r, 1)
                    act.activation(S[:, :, :], S[:, :, :], ACT.Exp).then_inc(e_r, 1)

                @block.vector
                def _(dve):
                    chain = Chain(dve, chain_s)
                    dve.tensor_copy(idx[:, :], const["runs"][:, bass.ds(b * 2, 2), :].rearrange("p f j -> p (f j)")).then_inc(idx_r, 1)
                    dve.memset(S[NS:P, NTL - 1, :], NEG)
                    dve.wait_ge(b_p, 1)
                    dve.tensor_copy(bT[:, 0:2 * GT_, :], pb[:, :, :]).then_inc(b_r, 1)
                    dve.wait_ge(b_pn, 1)
                    dve.tensor_copy(bT[0:NS, 2 * GT_, :], pm[0:NS, 0:DT]).then_inc(b_r, 1)
                    dve.wait_ge(b_r, 2)
                    dve.wait_ge(n_p, 1)
                    chain(dve.tensor_tensor(S[0:NS, NTL - 1, :].rearrange("p (r t) -> p r t", t=DT), pm[0:NS, 64:128].rearrange("p (r t) -> p r t", t=DT),
                                            bT[0:NS, 2 * GT_:2 * GT_ + 1, :].to_broadcast([NS, BH, DT]), ALU.add))
                    for m in range(0, 32, 2):
                        dve.wait_ge(kt_p, m + 1)
                        if m >= 2:
                            dve.wait_ge(s_p, m - 1)
                        dve.tensor_copy(kt[0][:, :, :], pt[0][:, :, :]).then_inc(kt_d, 1)
                        if m % 4 == 0 and m >= 4:
                            place_scores(dve, m // 4 - 1)
                    place_scores(dve, 7)
                    dve.wait_ge(s_r, 8)
                    dve.tensor_reduce(mx[:, :], S[:, :, :].rearrange("p n r -> p r n"), AX, ALU.max).then_inc(mx_r, 1)
                    dve.wait_ge(mxT_p, 1)
                    chain(dve.tensor_reduce(mr[:, 0:1], pm[0:NR, 128:256], AX, ALU.max))
                    chain(dve.tensor_scalar(mr[:, 1:2], mr[:, 0:1], -HD ** -0.5, None, ALU.mult))
                    dve.tensor_scalar(dg[:, :], ident[0:NR, 0:NR], mr[:, 1:2], None, ALU.mult).then_inc(dg_r, 1)
                    dve.wait_ge(nm_p, 1)
                    dve.scalar_tensor_tensor(out=S[:, :, :], in0=S[:, :, :], scalar=HD ** -0.5,
                                             in1=pm[:, 256:256 + NR].unsqueeze(1).to_broadcast([P, NTL, NR]), op0=ALU.mult, op1=ALU.add).then_inc(sub_r, 1)
                    dve.wait_ge(e_r, 1)
                    dve.tensor_reduce(dsum[:, :], S[:, :, :].rearrange("p n r -> p r n"), AX, ALU.add).then_inc(den_r, 1)
                    dve.wait_ge(den_p, 1)
                    chain(dve.reciprocal(mr[:, 2:3], pm[0:NR, 400:401]))
                    dve.wait_ge(o_p, 1)
                    chain(dve.tensor_tensor(om[:, :, :], po[:, :, :], const["masks"][0:NR, KV_OF, 0:KVH].unsqueeze(2).to_broadcast([NR, KVH, HD]), ALU.mult))
                    chain(dve.tensor_reduce(o[:, 0, :], om[:, :, :].rearrange("p k d -> p d k"), AX, ALU.add))
                    dve.tensor_scalar(o[:, 1, :], o[:, 0, :], mr[:, 2:3], None, ALU.mult).then_inc(y_r, 1)
            st.close_sems()


def stage_mix_out(nc, l, io, sc, const):
    with Stage(nc) as st:
        w = st.sb("w_out", [P, KT, D])
        g = st.sb("g_ffn", [P, D])
        x = st.sb("x_tile", [P, D])
        y = st.sb("y_tile", [P, D])
        xn = st.sb("xn", [P, D])
        sq = st.sb("sq", [P, D])
        yT = st.sb("yT", [P, KT, P])
        nT = st.sb("nT", [P, KT, P])
        stat = st.sb("stat", [P, 4])
        pm = [st.ps(f"pm{i}", [P, 512]) for i in range(2)]
        pt = [st.ps(f"pt{i}", [P, 4, P]) for i in range(4)]
        w_loaded = st.sem("w_loaded")
        with nc.Block() as block:
            @block.sync
            def _(sp):
                for k in range(KT):
                    sp.dma_start(w[:, k, :], layer(io["w_out"], l)[k * P:(k + 1) * P, :]).then_inc(w_loaded, 16)
                sp.dma_start(g[:, :], all_rows(layer(io["norm_ffn"], l)[0, :])).then_inc(w_loaded, 16)
                sp.wait_ge(w_loaded, 16 * (KT + 1))
        st.close_sems()
        with nc.Fori(0, TILES) as i:
            y_loaded = st.sem("y_loaded")
            x_loaded = st.sem("x_loaded")
            yT_psum = st.sem("yT_psum")
            yT_ready = st.sem("yT_ready")
            mixed = st.sem("mixed")
            x_new = st.sem("x_new")
            sumsq = st.sem("sumsq")
            root = st.sem("root")
            chain_s = st.sem("dve_chain")
            normed = st.sem("normed")
            nT_psum = st.sem("nT_psum")
            nT_ready = st.sem("nT_ready")
            stored = st.sem("stored")
            with nc.Block() as block:
                @block.sync
                def _(sp):
                    r = i * P
                    sp.dma_start(y[:, :], rows_at(sc["y"], r)).then_inc(y_loaded, 16)
                    sp.dma_start(x[:, :], rows_at(sc["x"], r)).then_inc(x_loaded, 16)
                    sp.wait_ge(x_new, 2)
                    sp.dma_start(rows_at(sc["x"], r), x[:, :]).then_inc(stored, 16)
                    sp.wait_ge(nT_ready, 2)
                    sp.dma_start(sc["nT"][:, :, bass.ds(r, P)], nT[:, :, :]).then_inc(stored, 16)
                    sp.wait_ge(stored, 32)

                @block.tensor
                def _(pe):
                    ident = const["ident"][:, :]
                    pe.wait_ge(y_loaded, 16)
                    for k in range(KT):
                        ins = pe.transpose(pt[k // 4][:, k % 4, :], y[:, k * P:(k + 1) * P], ident)
                        if k % 4 == 3:
                            ins.then_inc(yT_psum, 1)
                    pe.wait_ge(yT_ready, 2)
                    for n in range(2):
                        for k in range(KT):
                            ins = pe.matmul(pm[n][:, :], yT[:, k, :], w[:, k, n * 512:(n + 1) * 512],
                                            start=(k == 0), stop=(k == KT - 1))
                        ins.then_inc(mixed, 1)
                    pe.wait_ge(normed, 1)
                    for k in range(KT):
                        ins = pe.transpose(pt[2 + k // 4][:, k % 4, :], xn[:, k * P:(k + 1) * P], ident)
                        if k % 4 == 3:
                            ins.then_inc(nT_psum, 1)

                @block.scalar
                def _(act):
                    act.wait_ge(yT_psum, 2)
                    act.activation(yT[:, 4:8, :], pt[1][:, :, :], ACT.Copy).then_inc(yT_ready, 1)
                    act.wait_ge(x_new, 2)
                    act.activation(sq[:, :], x[:, :], ACT.Square, accum_out=stat[:, 0:1]).then_inc(sumsq, 1)
                    act.wait_ge(sumsq, 1)
                    act.activation(stat[:, 1:2], stat[:, 0:1], ACT.Sqrt, bias=const["eps"][:, 0:1], scale=1.0 / D).then_inc(root, 1)
                    act.wait_ge(nT_psum, 2)
                    act.activation(nT[:, 4:8, :], pt[3][:, :, :], ACT.Copy).then_inc(nT_ready, 1)

                @block.vector
                def _(dve):
                    chain = Chain(dve, chain_s)
                    dve.wait_ge(yT_psum, 1)
                    dve.tensor_copy(yT[:, 0:4, :], pt[0][:, :, :]).then_inc(yT_ready, 1)
                    dve.wait_ge(x_loaded, 16)
                    for n in range(2):
                        dve.wait_ge(mixed, n + 1)
                        c = slice(n * 512, (n + 1) * 512)
                        dve.tensor_tensor(x[:, c], pm[n][:, :], x[:, c], ALU.add).then_inc(x_new, 1)
                    dve.wait_ge(root, 1)
                    chain(dve.reciprocal(stat[:, 2:3], stat[:, 1:2]))
                    dve.wait_ge(x_new, 2)
                    dve.scalar_tensor_tensor(out=xn[:, :], in0=x[:, :], scalar=stat[:, 2:3], in1=g[:, :],
                                             op0=ALU.mult, op1=ALU.mult).then_inc(normed, 1)
                    dve.wait_ge(nT_psum, 1)
                    dve.tensor_copy(nT[:, 0:4, :], pt[2][:, :, :]).then_inc(nT_ready, 1)
            st.close_sems()


FF_COLS = ((0, 512), (512, 512), (1024, 128))


def stage_ffn_up(nc, l, io, sc, const):
    with Stage(nc) as st:
        nT = st.sb("nT", [P, KT, ROWS])
        wb = [st.sb(f"wgu{b}", [P, 2, KT, P]) for b in range(2)]
        e = st.sb("exp_neg", [P, 512])
        sg = st.sb("sig", [P, 512])
        gate = st.sb("gate", [P, 512])
        h = [st.sb(f"hT{b}", [P, ROWS]) for b in range(2)]
        pg = [st.ps(f"pg{i}", [P, 512]) for i in range(3)]
        pu = [st.ps(f"pu{i}", [P, 512]) for i in range(3)]

        def weights(which, f):
            return layer(io[which], l)[:, bass.ds(f * P, P)].rearrange("(k p) n -> p k n", p=P)

        loaded = st.sem("loaded")
        with nc.Block() as block:
            @block.sync
            def _(sp):
                sp.dma_start(nT[:, :, :], sc["nT"]).then_inc(loaded, 16)
                for k, which in enumerate(("w_gate", "w_up")):
                    sp.dma_start(wb[0][:, k, :, :], weights(which, 0)).then_inc(loaded, 16)
                sp.wait_ge(loaded, 48)
        st.close_sems()
        with nc.Fori(0, FT - 1, 2) as f:
            w1_loaded = st.sem("w1_loaded")
            w0_loaded = st.sem("w0_loaded")
            gate_done = st.sem("gate_done")
            up_done = st.sem("up_done")
            exped = st.sem("exped")
            gate_out = st.sem("gate_out")
            hid = st.sem("hid")
            chain_s = st.sem("dve_chain")
            stored = st.sem("stored")
            with nc.Block() as block:
                @block.sync
                def _(sp):
                    for k, which in enumerate(("w_gate", "w_up")):
                        sp.dma_start(wb[1][:, k, :, :], weights(which, f + 1)).then_inc(w1_loaded, 16)
                    sp.wait_ge(up_done, 3)
                    for k, which in enumerate(("w_gate", "w_up")):
                        sp.dma_start(wb[0][:, k, :, :], weights(which, (f + 2) % FT)).then_inc(w0_loaded, 16)
                    for b in range(2):
                        sp.wait_ge(hid, 3 * (b + 1))
                        sp.dma_start(sc["hT"][bass.ds(f + b, 1), :, :].rearrange("o p n -> (o p) n"), h[b][:, :]).then_inc(stored, 16)
                    sp.wait_ge(w0_loaded, 32)
                    sp.wait_ge(stored, 32)

                @block.tensor
                def _(pe):
                    for b in range(2):
                        if b == 1:
                            pe.wait_ge(w1_loaded, 32)
                        for n, (c0, cw) in enumerate(FF_COLS):
                            m = 3 * b + n
                            if b == 1:
                                pe.wait_ge(hid, m - 2)
                            for k in range(KT):
                                ins = pe.matmul(pg[n][:, 0:cw], wb[b][:, 0, k, :], nT[:, k, c0:c0 + cw], start=(k == 0), stop=(k == KT - 1))
                            ins.then_inc(gate_done, 1)
                            for k in range(KT):
                                ins = pe.matmul(pu[n][:, 0:cw], wb[b][:, 1, k, :], nT[:, k, c0:c0 + cw], start=(k == 0), stop=(k == KT - 1))
                            ins.then_inc(up_done, 1)

                @block.scalar
                def _(act):
                    for m in range(6):
                        c0, cw = FF_COLS[m % 3]
                        act.wait_ge(gate_done, m + 1)
                        if m:
                            act.wait_ge(hid, m)
                        act.activation(e[:, 0:cw], pg[m % 3][:, 0:cw], ACT.Exp, scale=-1.0).then_inc(exped, 1)
                        act.activation(gate[:, 0:cw], pg[m % 3][:, 0:cw], ACT.Copy).then_inc(gate_out, 1)

                @block.vector
                def _(dve):
                    chain = Chain(dve, chain_s)
                    for m in range(6):
                        c0, cw = FF_COLS[m % 3]
                        dve.wait_ge(exped, m + 1)
                        chain(dve.tensor_scalar(sg[:, 0:cw], e[:, 0:cw], 1.0, None, ALU.add))
                        chain(dve.reciprocal(e[:, 0:cw], sg[:, 0:cw]))
                        dve.wait_ge(gate_out, m + 1)
                        chain(dve.tensor_tensor(sg[:, 0:cw], gate[:, 0:cw], e[:, 0:cw], ALU.mult))
                        dve.wait_ge(up_done, m + 1)
                        dve.tensor_tensor(h[m // 3][:, c0:c0 + cw], pu[m % 3][:, 0:cw], sg[:, 0:cw], ALU.mult).then_inc(hid, 1)
            st.close_sems()


def stage_ffn_down(nc, l, io, sc, const):
    with Stage(nc) as st:
        w = st.sb("w_down", [P, FT, D])
        h = [st.sb(f"hT{b}", [P, FT, P]) for b in range(2)]
        x = st.sb("x_tile", [P, D])
        pm = [st.ps(f"pm{i}", [P, 512]) for i in range(2)]
        loaded = st.sem("loaded")
        hT = sc["hT"].rearrange("f p n -> p f n")
        with nc.Block() as block:
            @block.sync
            def _(sp):
                sp.dma_start(h[0][:, :, :], hT[:, :, 0:P]).then_inc(loaded, 16)
                for k in range(0, FT, 2):
                    sp.dma_start(w[:, k:k + 2, :], layer(io["w_down"], l)[k * P:(k + 2) * P, :].rearrange("(k p) n -> p k n", p=P)).then_inc(loaded, 16)
                sp.wait_ge(loaded, 16 * (1 + FT // 2))
        st.close_sems()

        def body(i, b, more):
            h_next = st.sem("h_next")
            x_loaded = st.sem("x_loaded")
            down = st.sem("down")
            x_new = st.sem("x_new")
            stored = st.sem("stored")
            with nc.Block() as block:
                @block.sync
                def _(sp):
                    r = i * P
                    sp.dma_start(x[:, :], rows_at(sc["x"], r)).then_inc(x_loaded, 16)
                    if more:
                        sp.dma_start(h[1 - b][:, :, :], hT[:, :, bass.ds(r + P, P)]).then_inc(h_next, 16)
                    sp.wait_ge(x_new, 2)
                    sp.dma_start(rows_at(sc["x"], r), x[:, :]).then_inc(stored, 16)
                    sp.wait_ge(stored, 16)
                    if more:
                        sp.wait_ge(h_next, 16)

                @block.tensor
                def _(pe):
                    for n in range(2):
                        for k in range(FT):
                            ins = pe.matmul(pm[n][:, :], h[b][:, k, :], w[:, k, n * 512:(n + 1) * 512],
                                            start=(k == 0), stop=(k == FT - 1))
                        ins.then_inc(down, 1)

                @block.vector
                def _(dve):
                    dve.wait_ge(x_loaded, 16)
                    for n in range(2):
                        dve.wait_ge(down, n + 1)
                        c = slice(n * 512, (n + 1) * 512)
                        dve.tensor_tensor(x[:, c], pm[n][:, :], x[:, c], ALU.add).then_inc(x_new, 1)
            st.close_sems()

        with nc.Fori(0, NT - 1, 2) as i:
            body(i, 0, True)
            body(i + 1, 1, True)
        body(NT, 0, False)


def stage_final(nc, io, sc, const):
    with Stage(nc) as st:
        x = st.sb("x_tile", [P, D])
        g = st.sb("g_final", [P, D])
        sq = st.sb("sq", [P, D])
        stat = st.sb("stat", [P, 4])

        def body(i, rows, out):
            x_loaded = st.sem("x_loaded")
            sumsq = st.sem("sumsq")
            root = st.sem("root")
            chain_s = st.sem("dve_chain")
            normed = st.sem("normed")
            stored = st.sem("stored")
            with nc.Block() as block:
                @block.sync
                def _(sp):
                    sp.dma_start(x[:, :], rows_at(sc["x"], i * P)).then_inc(x_loaded, 16)
                    sp.dma_start(g[:, :], all_rows(io["norm_final"])).then_inc(x_loaded, 16)
                    sp.wait_ge(normed, 1)
                    sp.dma_start(out, sq[0:rows, :]).then_inc(stored, 16)
                    sp.wait_ge(stored, 16)

                @block.scalar
                def _(act):
                    act.wait_ge(x_loaded, 32)
                    act.activation(sq[:, :], x[:, :], ACT.Square, accum_out=stat[:, 0:1]).then_inc(sumsq, 1)
                    act.wait_ge(sumsq, 1)
                    act.activation(stat[:, 1:2], stat[:, 0:1], ACT.Sqrt, bias=const["eps"][:, 0:1], scale=1.0 / D).then_inc(root, 1)

                @block.vector
                def _(dve):
                    chain = Chain(dve, chain_s)
                    dve.wait_ge(root, 1)
                    chain(dve.reciprocal(stat[:, 2:3], stat[:, 1:2]))
                    dve.scalar_tensor_tensor(out=sq[:, :], in0=x[:, :], scalar=stat[:, 2:3], in1=g[:, :],
                                             op0=ALU.mult, op1=ALU.mult).then_inc(normed, 1)
            st.close_sems()

        with nc.Fori(0, NT) as i:
            body(i, P, rows_at(io["y_prompt"].rearrange("b t n -> (b t) n"), i * P))
        body(NT, NS, io["y_sample"].rearrange("b t n -> (b t) n"))


INPUTS = ['x_prompt', 'x_sample', 'cache_k', 'cache_v', 'cache_idx_k', 'state_mlstm_C', 'state_mlstm_n',
          'state_mlstm_m', 'state_rwkv_shift', 'state_rwkv_S', 'page_table', 'norm_mix', 'w_in', 'mlstm_gate_b',
          'mlstm_norm', 'rwkv_mu', 'rwkv_w0', 'rwkv_w2', 'rwkv_a0', 'rwkv_a2', 'rwkv_g2', 'rwkv_k_k', 'rwkv_k_a',
          'rwkv_r_k', 'rwkv_ln_w', 'rwkv_ln_b', 'w_out', 'norm_ffn', 'w_gate', 'w_up', 'w_down', 'norm_final']
OUTPUTS = [('y_prompt', (1, SEQ, D)), ('y_sample', (DB, DT, D))]
for _p, _b, _t in (('p', 1, SEQ), ('s', DB, DT)):
    OUTPUTS += [(f'{_p}_k', (DEPTH, _b, _t, KVH, HD)), (f'{_p}_v', (DEPTH, _b, _t, KVH, HD)),
                (f'{_p}_idx_k', (DEPTH, _b, _t, HD)), (f'{_p}_mlstm_C', (DEPTH, _b, AH, HD, HD)),
                (f'{_p}_mlstm_n', (DEPTH, _b, AH, HD)), (f'{_p}_mlstm_m', (DEPTH, _b, AH)),
                (f'{_p}_rwkv_shift', (DEPTH, _b, C_PROJ)), (f'{_p}_rwkv_S', (DEPTH, _b, CH, HD, HD))]


def stage_start(nc, io, sc, const):
    with Stage(nc) as st:
        made = st.sem("made")
        filled = st.sem("filled")
        laid = st.sem("laid")
        with nc.Block() as block:
            @block.vector
            def _(dve):
                dve.memset(const["zeros"][:, :], 0.0).then_inc(made, 1)
                dve.memset(const["eps"][:, :], EPS).then_inc(filled, 1)
                dve.memset(const["ones"][:, :], 1.0).then_inc(filled, 1)
                dve.memset(const["lneps"][:, :], LN_EPS).then_inc(filled, 1)
                dve.memset(const["lbase"][:, :], 0.0).then_inc(filled, 1)

            @block.sync
            def _(sp):
                sp.dma_start(sc["x"][0:SEQ, :], io["x_prompt"].rearrange("b t n -> (b t) n")).then_inc(laid, 16)
                sp.dma_start(sc["x"][SEQ:SEQ + NS, :], io["x_sample"].rearrange("b t n -> (b t) n")).then_inc(laid, 16)
                sp.dma_start(const["ident"][:, :], io["ident"]).then_inc(laid, 16)
                sp.dma_start(const["masks"][:, :, :], io["masks"].rearrange("m p n -> p m n")).then_inc(laid, 16)
                sp.dma_start(const["sub"][:, :], io["sub"]).then_inc(laid, 16)
                sp.wait_ge(made, 1)
                sp.dma_start(sc["x"][SEQ + NS:ROWS, :], const["zeros"][0:P - NS, 0:D]).then_inc(laid, 16)
                sp.dma_start(sc["y"][SEQ + NS:ROWS, :], const["zeros"][0:P - NS, 0:D]).then_inc(laid, 16)
                sp.wait_ge(laid, 112)


def build(nc, io):
    sc = {}
    for name, shape in (("x", (ROWS, D)), ("pa", (ROWS, A_PROJ)), ("v", (ROWS, KVH * HD)), ("iw", (ROWS, IH)),
                        ("pc", (ROWS, C_PROJ)), ("prev", (ROWS + 1, C_PROJ)), ("k", (ROWS, KVH * HD)),
                        ("ik", (ROWS, HD)), ("qT", (4, P, ROWS)), ("iqT", (4, P, ROWS)), ("kT", (2, P, ROWS)),
                        ("ikT", (P, ROWS)), ("y", (ROWS, D)),
                        ("nT", (P, KT, ROWS)), ("hT", (FT, P, ROWS)),
                        ("score", (P, HALF)), ("score_new", (NS, NS)), ("bias", (P, HALF)), ("bias_new", (NS, NS))):
        sc[name] = nc.dram_tensor("scratch_" + name, shape, F32).ap()
    with ExitStack() as ctx:
        const = {}
        for name, shape in (("ident", [P, P]), ("zeros", [P, D]), ("eps", [P, 1]), ("ones", [P, P]), ("lneps", [P, 1]),
                            ("masks", [P, NMASK, P])):
            const[name] = ctx.enter_context(nc.sbuf_tensor("c_" + name, shape, F32))
        const["lbase"] = ctx.enter_context(nc.sbuf_tensor("c_lbase", [P, 1], F32))
        const["sub"] = ctx.enter_context(nc.sbuf_tensor("c_sub", [P, 2], F32))
        const["runs"] = ctx.enter_context(nc.sbuf_tensor("c_runs", [P, 2 * DB, 2], U32))
        stage_start(nc, io, sc, const)
        with nc.Fori(0, DEPTH) as l:
            stage_project(nc, l, io, sc, const)
            stage_mlstm(nc, l, io, sc, const)
            stage_rwkv(nc, l, io, sc, const)
            stage_prompt_dsa(nc, l, io, sc, const)
            stage_sample_index(nc, l, io, sc, const)
            stage_sample_select(nc, l, io, sc, const)
            stage_sample_attend(nc, l, io, sc, const)
            stage_mix_out(nc, l, io, sc, const)
            stage_ffn_up(nc, l, io, sc, const)
            stage_ffn_down(nc, l, io, sc, const)
        stage_final(nc, io, sc, const)



def rope_table():
    half = 8
    inv = (500000.0 ** (-np.arange(half, dtype=np.float32) / half)).astype(np.float32)
    pos = np.concatenate([np.arange(SEQ), PAST + np.arange(NS) % DT, np.zeros(P - NS)]).astype(np.float32)
    ang = (pos[:, None] * inv[None, :]).astype(np.float32)
    return np.concatenate([np.cos(ang), np.sin(ang)], axis=1).astype(np.float32)


def mask_tables():
    s = np.arange(P)[:, None]
    t = np.arange(P)[None, :]
    out = []
    out.append(np.where(s <= t, 0.0, NEG))
    same8 = (s // DT == t // DT)
    out.append(np.where((s <= t) & same8, 0.0, NEG))
    for c in (CHUNK, DT):
        same = (s // c == t // c)
        out += [(same & (s < t)) * 1.0, (same & (s <= t)) * 1.0, (same & (s > t)) * 1.0]
    out.append(np.where(s >= t, 0.0, NEG))
    out.append(np.where((s >= t) & same8, 0.0, NEG))
    for n in (1, 2, 4, 8, 16, 32):
        out.append(((s // (2 * n) == t // (2 * n)) & (s // n % 2 == 1) & (t // n % 2 == 0)) * 1.0)
    for n in (1, 2, 4, 8, 16, 32):
        out.append(out[LEVEL_TS + int(math.log2(n))].T)
    sel = np.zeros((P, P))
    for f in range(2):
        for h in range(IH):
            for tt in range(DT):
                sel[f * 64 + h * 8 + tt, f * 8 + tt] = 1.0
    out.append(sel)
    out.append((s // DT == t) * 1.0)
    out.append((s // CHUNK == t) * 1.0)
    out.append((s // (2 * DT) == t) * 1.0)
    return np.stack(out).astype(np.float32)


CAUSAL_ST, CAUSAL_ST8, STRICT64, INCL64, LOWER64, STRICT8, INCL8, LOWER8, CAUSAL_QK, CAUSAL_QK8 = range(10)
LEVEL_TS = 10
LEVEL_ST = 16
PICK = 22
SEQ_OF = 23
CHUNK_OF = 24
KV_OF = 25
NMASK = 26


def kernel(**inputs):
    import concourse.bacc as _bacc
    from concourse.bass_utils import run_bass_kernel_spmd as _run

    nc = _bacc.Bacc("TRN2", target_bir_lowering=False, num_devices=1)
    arrays, io = {}, {}
    host = {name: np.ascontiguousarray(inputs[name]) for name in INPUTS}
    host["rope"] = rope_table()
    host["ident"] = np.eye(P, dtype=np.float32)
    host["masks"] = mask_tables()
    pages = np.asarray(inputs["page_table"]).reshape(DB, 2, NPAGES // 2).transpose(2, 0, 1).reshape(NPAGES // 2, 1, 2 * DB)
    host["pages"] = np.ascontiguousarray(np.broadcast_to(pages, (NPAGES // 2, 4, 2 * DB)).reshape(P, 2 * DB))
    host["sub"] = (np.arange(P)[:, None] % 4 + 4 * np.arange(2)[None, :]).astype(np.float32)
    for name, a in host.items():
        arrays["in_" + name] = a
        io[name] = nc.dram_tensor("in_" + name, a.shape, mybir.dt.from_np(a.dtype), kind="ExternalInput").ap()
    for name, shape in OUTPUTS:
        io[name] = nc.dram_tensor("out_" + name, shape, F32, kind="ExternalOutput").ap()
    build(nc, io)
    r = _run(nc, [arrays], core_ids=[0])
    return tuple(r.results[0]["out_" + name] for name, _ in OUTPUTS)
```
